# Optimizing a Trainium2 kernel written in Bass

```python
import math
import jax, jax.numpy as jnp
from jax import lax
import numpy as np

D_MODEL = 2048
BATCH = 1
SEQ = 256
DEPTH = 2

N_EVEN = (DEPTH + 1) // 2
N_ODD = DEPTH // 2
EPS = 1e-6

DA_WIDTH = D_MODEL // 2
DA_HEADS = 8
DA_HEAD_DIM = DA_WIDTH // DA_HEADS // 2
DA_V_DIM = 2 * DA_HEAD_DIM
ROPE_DIM = DA_HEAD_DIM // 4
ROPE_THETA = 500000.0
Q_BLOCK = 128

RW_WIDTH = D_MODEL // 2
RW_HEAD = 64
RW_HEADS = RW_WIDTH // RW_HEAD
DECAY_LORA = 64
AAA_LORA = 64
GATE_LORA = 32
RW_IN = 3 * RW_WIDTH + DECAY_LORA + AAA_LORA + GATE_LORA
RW_GN_EPS = 64e-5

EVEN_IN = 3 * DA_WIDTH + RW_IN
EVEN_OUT = DA_WIDTH + RW_WIDTH

HG_EXPAND = 128
HG_HEADS = D_MODEL // HG_EXPAND
HG_HEAD_DIM = D_MODEL // HG_HEADS
HG_CHUNK = 64
ODD_IN = 4 * D_MODEL

FFN_HIDDEN = -(-8 * D_MODEL // (3 * 256)) * 256

kernel_name = "hybrid_diffattn_rwkv7_hgrn2_swiglu"

def rms_norm(x, g, eps=EPS):
    xf = x.astype(jnp.float32)
    y = xf * lax.rsqrt(jnp.mean(xf * xf, axis=-1, keepdims=True) + eps)
    return (y * g).astype(x.dtype)

def partial_rope(x, cos, sin):
    half = ROPE_DIM // 2
    x1, x2, xp = x[..., :half], x[..., half:ROPE_DIM], x[..., ROPE_DIM:]
    return jnp.concatenate([x1 * cos - x2 * sin, x2 * cos + x1 * sin, xp], axis=-1).astype(x.dtype)

def diff_attention(qa, ka, va, lam_vec, subln_g, lam_init):
    B, S, _ = qa.shape
    pos = jnp.arange(S, dtype=jnp.float32)
    inv_freq = 1.0 / (ROPE_THETA ** (jnp.arange(0, ROPE_DIM, 2, dtype=jnp.float32) / ROPE_DIM))
    ang = pos[:, None] * inv_freq[None, :]
    cos = jnp.cos(ang)[:, None, None, :]
    sin = jnp.sin(ang)[:, None, None, :]
    q = partial_rope(qa.reshape(B, S, DA_HEADS, 2, DA_HEAD_DIM), cos, sin).transpose(0, 2, 3, 1, 4)
    k = partial_rope(ka.reshape(B, S, DA_HEADS, 2, DA_HEAD_DIM), cos, sin).transpose(0, 2, 3, 1, 4)
    v = va.reshape(B, S, DA_HEADS, DA_V_DIM).transpose(0, 2, 1, 3)
    lf = lam_vec.astype(jnp.float32)
    lam = jnp.exp(jnp.sum(lf[0] * lf[1])) - jnp.exp(jnp.sum(lf[2] * lf[3])) + lam_init
    scale = DA_HEAD_DIM ** -0.5
    outs = []
    for blk in range(S // Q_BLOCK):
        q0 = blk * Q_BLOCK
        kend = q0 + Q_BLOCK
        s = jnp.einsum('bhcqd,bhckd->bhcqk', q[:, :, :, q0:kend], k[:, :, :, :kend]).astype(jnp.float32) * scale
        mask = jnp.arange(kend)[None, :] <= (q0 + jnp.arange(Q_BLOCK))[:, None]
        p = jax.nn.softmax(jnp.where(mask, s, -jnp.inf), axis=-1)
        w = p[:, :, 0] - lam * p[:, :, 1]
        outs.append(jnp.einsum('bhqk,bhkv->bhqv', w.astype(v.dtype), v[:, :, :kend]))
    o = jnp.concatenate(outs, axis=2)
    o = rms_norm(o, subln_g) * (1.0 - lam_init)
    return o.transpose(0, 2, 1, 3).reshape(B, S, DA_WIDTH)

def rwkv7_time_mix(p, mu, w0, w_up, a0, a_up, g_up, k_k, k_a, r_k, ln_w, ln_b):
    B, S, _ = p.shape
    prev = jnp.pad(p, ((0, 0), (1, 0), (0, 0)))[:, :-1]
    xm = p + (prev - p) * mu
    c = [RW_WIDTH, 2 * RW_WIDTH, 3 * RW_WIDTH, 3 * RW_WIDTH + DECAY_LORA, 3 * RW_WIDTH + DECAY_LORA + AAA_LORA]
    r, k, v, wl, al, gl = jnp.split(xm, c, axis=-1)
    w_log = -jax.nn.softplus(-(w0 + jnp.tanh(wl) @ w_up)) - 0.5
    decay = jnp.exp(-jnp.exp(w_log.astype(jnp.float32)))
    a = jax.nn.sigmoid(a0 + al @ a_up)
    g = jax.nn.sigmoid(gl) @ g_up
    heads = lambda t: t.reshape(B, S, RW_HEADS, RW_HEAD)
    kk = heads(k * k_k).astype(jnp.float32)
    kk = kk / jnp.maximum(jnp.linalg.norm(kk, axis=-1, keepdims=True), 1e-12)
    k = k * (1.0 + (a - 1.0) * k_a)
    r_h, k_h, v_h, a_h, w_h = heads(r), heads(k), heads(v), heads(a), heads(decay)
    xs = tuple(t.astype(jnp.float32).transpose(1, 0, 2, 3) for t in (r_h, w_h, k_h, v_h, kk, a_h))

    def step(state, inp):
        rt, wt, kt, vt, kkt, at = inp
        sa = jnp.einsum('bhvk,bhk->bhv', state, -kkt)
        state = state * wt[:, :, None, :] + sa[..., None] * (kkt * at)[:, :, None, :] + vt[..., None] * kt[:, :, None, :]
        return state, jnp.einsum('bhvk,bhk->bhv', state, rt)

    init = jnp.zeros((B, RW_HEADS, RW_HEAD, RW_HEAD), jnp.float32)
    _, y = lax.scan(step, init, xs)
    y = y.transpose(1, 0, 2, 3)
    mean = jnp.mean(y, axis=-1, keepdims=True)
    var = jnp.mean(jnp.square(y - mean), axis=-1, keepdims=True)
    yn = ((y - mean) * lax.rsqrt(var + RW_GN_EPS)).reshape(B, S, RW_WIDTH) * ln_w + ln_b
    bonus = (jnp.sum(r_h * k_h * r_k, axis=-1, keepdims=True) * v_h).reshape(B, S, RW_WIDTH)
    return ((yn + bonus) * g).astype(p.dtype)

def hgrn2(p, lb, norm_g):
    B, S, _ = p.shape
    q, f, i, g = jnp.split(p, 4, axis=-1)
    f = lb + (1.0 - lb) * jax.nn.sigmoid(f.astype(jnp.float32))
    log_f = jnp.log(f)
    k = 1.0 - f
    n = S // HG_CHUNK
    chunks = lambda t: t.astype(jnp.float32).reshape(B, n, HG_CHUNK, HG_HEADS, -1).transpose(1, 0, 3, 2, 4)
    mask = jnp.tril(jnp.ones((HG_CHUNK, HG_CHUNK), bool))

    def step(state, inp):
        qc, kc, ic, lfc = inp
        b = jnp.cumsum(lfc, axis=-2)
        o_inter = jnp.einsum('bhtd,bhdv->bhtv', qc * jnp.exp(b), state)
        decay = jnp.exp(jnp.where(mask[:, :, None], b[:, :, :, None, :] - b[:, :, None, :, :], -jnp.inf))
        attn = jnp.einsum('bhtd,bhsd,bhtsd->bhts', qc, kc, decay)
        o = o_inter + jnp.einsum('bhts,bhsv->bhtv', attn, ic)
        b_last = b[:, :, -1:, :]
        state = jnp.exp(b_last[:, :, 0, :])[..., None] * state + jnp.einsum('bhsd,bhsv->bhdv', kc * jnp.exp(b_last - b), ic)
        return state, o

    init = jnp.zeros((B, HG_HEADS, HG_EXPAND, HG_HEAD_DIM), jnp.float32)
    _, o = lax.scan(step, init, (chunks(q), chunks(k), chunks(i), chunks(log_f)))
    o = o.transpose(1, 0, 3, 2, 4).reshape(B, S, HG_HEADS, HG_HEAD_DIM)
    o = rms_norm(o, norm_g).reshape(B, S, D_MODEL) * jax.nn.silu(g)
    return o.astype(p.dtype)

def setup_inputs(seed: int = 0) -> dict:
    key = jax.random.key(seed)
    ks = iter(list(jax.random.split(key, 32)))
    nrm = lambda shape, scale: jax.random.normal(next(ks), shape, jnp.float32) * scale
    gain = lambda shape: 1.0 + nrm(shape, 0.02)
    D = D_MODEL
    return {
        "x": nrm((BATCH, SEQ, D), 1.0),
        "attn_norm_g": gain((DEPTH, D)),
        "ffn_norm_g": gain((DEPTH, D)),
        "final_norm_g": gain((D,)),
        "even_w_in": nrm((N_EVEN, D, EVEN_IN), D ** -0.5),
        "even_w_out": nrm((N_EVEN, EVEN_OUT, D), EVEN_OUT ** -0.5),
        "da_lambda": nrm((N_EVEN, 4, DA_HEAD_DIM), 0.1),
        "da_subln_g": gain((N_EVEN, DA_V_DIM)),
        "rw_mu": jax.random.uniform(next(ks), (N_EVEN, RW_IN), jnp.float32),
        "rw_w0": jax.random.uniform(next(ks), (N_EVEN, RW_WIDTH), jnp.float32, minval=-6.5, maxval=-1.5),
        "rw_w_up": nrm((N_EVEN, DECAY_LORA, RW_WIDTH), 0.1 * DECAY_LORA ** -0.5),
        "rw_a0": nrm((N_EVEN, RW_WIDTH), 0.1),
        "rw_a_up": nrm((N_EVEN, AAA_LORA, RW_WIDTH), 0.5 * AAA_LORA ** -0.5),
        "rw_g_up": nrm((N_EVEN, GATE_LORA, RW_WIDTH), GATE_LORA ** -0.5),
        "rw_k_k": 0.85 + nrm((N_EVEN, RW_WIDTH), 0.02),
        "rw_k_a": gain((N_EVEN, RW_WIDTH)),
        "rw_r_k": nrm((N_EVEN, RW_HEADS, RW_HEAD), 0.1),
        "rw_ln_w": gain((N_EVEN, RW_WIDTH)),
        "rw_ln_b": nrm((N_EVEN, RW_WIDTH), 0.01),
        "odd_w_in": nrm((N_ODD, D, ODD_IN), D ** -0.5),
        "odd_w_out": nrm((N_ODD, D, D), D ** -0.5),
        "hg_lower_bound": nrm((DEPTH, D), 1.0),
        "hg_norm_g": gain((N_ODD, HG_HEAD_DIM)),
        "ffn_w_gate": nrm((DEPTH, D, FFN_HIDDEN), D ** -0.5),
        "ffn_w_up": nrm((DEPTH, D, FFN_HIDDEN), D ** -0.5),
        "ffn_w_down": nrm((DEPTH, FFN_HIDDEN, D), FFN_HIDDEN ** -0.5),
    }

def reference(x, attn_norm_g, ffn_norm_g, final_norm_g, even_w_in, even_w_out, da_lambda, da_subln_g,
              rw_mu, rw_w0, rw_w_up, rw_a0, rw_a_up, rw_g_up, rw_k_k, rw_k_a, rw_r_k, rw_ln_w, rw_ln_b,
              odd_w_in, odd_w_out, hg_lower_bound, hg_norm_g, ffn_w_gate, ffn_w_up, ffn_w_down):
    s_lb = jax.nn.softmax(hg_lower_bound.astype(jnp.float32), axis=0)
    lb_all = jnp.cumsum(s_lb, axis=0) - s_lb[0]
    for layer in range(DEPTH):
        j = layer // 2
        h = rms_norm(x, attn_norm_g[layer])
        if layer % 2 == 0:
            p = h @ even_w_in[j]
            qa, ka, va = jnp.split(p[..., :3 * DA_WIDTH], 3, axis=-1)
            lam_init = 0.8 - 0.6 * math.exp(-0.3 * layer)
            a_out = diff_attention(qa, ka, va, da_lambda[j], da_subln_g[j], lam_init)
            b_out = rwkv7_time_mix(p[..., 3 * DA_WIDTH:], rw_mu[j], rw_w0[j], rw_w_up[j], rw_a0[j], rw_a_up[j],
                                   rw_g_up[j], rw_k_k[j], rw_k_a[j], rw_r_k[j], rw_ln_w[j], rw_ln_b[j])
            mix = jnp.concatenate([a_out, b_out.astype(a_out.dtype)], axis=-1) @ even_w_out[j]
        else:
            p = h @ odd_w_in[j]
            mix = hgrn2(p, lb_all[layer], hg_norm_g[j]) @ odd_w_out[j]
        x = x + mix.astype(x.dtype)
        h = rms_norm(x, ffn_norm_g[layer])
        x = x + ((jax.nn.silu(h @ ffn_w_gate[layer]) * (h @ ffn_w_up[layer])) @ ffn_w_down[layer]).astype(x.dtype)
    return rms_norm(x, final_norm_g)


_drawn_inputs = setup_inputs


def setup_inputs(seed=0):
    import zlib

    import numpy as np

    out = dict(_drawn_inputs(seed))
    spreads = {}
    factors = {'ffn_norm_g': 2.744,
     'final_norm_g': 2.94,
     'da_subln_g': 3.776,
     'rw_w_up': 8.0,
     'rw_a0': 2.874,
     'rw_k_k': 7.378,
     'rw_k_a': 5.749,
     'rw_ln_w': 6.233,
     'rw_ln_b': 8.0,
     'hg_norm_g': 7.559}
    for name, (base, spread) in spreads.items():
        noise = np.random.default_rng([zlib.crc32(name.encode()), seed]).standard_normal(out[name].shape)
        drawn = base * np.exp(spread * noise) if base else spread * noise
        out[name] = __import__('jax').numpy.asarray(drawn.astype(out[name].dtype))
    for name, factor in factors.items():
        out[name] = (out[name] * factor).astype(out[name].dtype)
    return out
```

```python
from contextlib import ExitStack
import math

import numpy as np
import concourse.bass as bass
from concourse import mybir

F32 = mybir.dt.float32
F32R = mybir.dt.float32r
ACT = mybir.ActivationFunctionType
ALU = mybir.AluOpType
AX = mybir.AxisListType

P = 128
D = 2048
T = 256
KT = D // P
NRW = 8
NHG = 16
FB = 44
PASSES = (16, 16, 12)
EPS = 1e-6
GN_EPS = 64e-5
RAW, RES = 4, 2
HALF = KT // 2
LEVELS = 7
LAM_INIT = 0.8 - 0.6 * math.exp(0.0)
NEG_EXP_HALF = -math.exp(-0.5)
LOG_SHIFT = 24

C_ONES, C_HEAD, C_ROT = 0, 128, 256
C_LVL = 384
C_ID = C_LVL + LEVELS * P
C_TRI = C_ID + P
C_LOW0 = C_TRI + 2 * P
C_COS = C_LOW0 + P
C_SIN = C_COS + T
C_CAUSAL = C_SIN + T
C_END = C_CAUSAL + 3 * P
P_MU, P_W0, P_A0, P_KK, P_KA, P_RK = 0, 3, 4, 5, 6, 7
NPAR = 8
G_ATT0, G_FFN0, G_ATT1, G_FFN1, G_FIN = 0, 16, 32, 48, 64
G_LB0, G_LB1 = 80, 96
G_SUB, G_HGN, G_MUW, G_MUG = 112, 113, 114, 115
G_LAM = 116
NG = G_LAM + 256


def shape_constants():
    c = np.zeros((P, C_END), np.float32)
    i = np.arange(P)
    c[:, C_ID:C_ID + P] = np.eye(P)
    c[:, C_ONES:C_ONES + P] = 1.0
    c[:, C_HEAD:C_HEAD + P] = (i[:, None] // 64 == i[None, :] // 64)
    for comp in range(2):
        for d in range(8):
            c[64 * comp + d + 8, C_ROT + 64 * comp + d] = -1.0
            c[64 * comp + d, C_ROT + 64 * comp + d + 8] = 1.0
    s, t = i[:, None], i[None, :]
    for l in range(LEVELS):
        b = 1 << l
        m = (s // (2 * b) == t // (2 * b)) & ((s // b) % 2 == 0) & ((t // b) % 2 == 1)
        c[:, C_LVL + l * P:C_LVL + (l + 1) * P] = m
        if l == 0:
            c[:, C_LOW0:C_LOW0 + P] = m.T
    c[:, C_TRI:C_TRI + P] = s < t
    c[:, C_TRI + P:C_TRI + 2 * P] = s <= t
    inv = (1.0 / (np.float32(500000.0) ** (np.arange(0, 16, 2, dtype=np.float32) / np.float32(16)))).astype(np.float32)
    ang = (np.arange(T, dtype=np.float32)[None, :] * inv[:, None]).astype(np.float32)
    c[:, C_COS:C_COS + T] = 1.0
    for comp in range(2):
        for half in range(2):
            r = 64 * comp + 8 * half
            c[r:r + 8, C_COS:C_COS + T] = np.cos(ang)
            c[r:r + 8, C_SIN:C_SIN + T] = np.sin(ang)
    low = np.where(i[None, :] <= i[:, None], 0.0, -1e30)
    c[:, C_CAUSAL:C_CAUSAL + P] = low
    c[:, C_CAUSAL + 2 * P:C_CAUSAL + 3 * P] = low
    return c


def build(nc, xT, w_even, w_even_out, w_odd, w_odd_out, w_gu, w_down, consts, gains, par, par_ln, wa_up, g_up, out):
    with ExitStack() as ctx:
        def sb(name, shape, dt=F32):
            return ctx.enter_context(nc.sbuf_tensor(name, shape, dt))

        def sem(name):
            return ctx.enter_context(nc.semaphore(name))

        raw = sb("w_raw", [P, RAW, KT, P])
        wh = sb("w_high", [P, RES, KT, P], F32R)
        wl = sb("w_low", [P, RES, KT, P], F32R)
        hh = sb("h_high", [P, KT, T], F32R)
        hl = sb("h_low", [P, KT, T], F32R)
        mh = sb("mix_high", [P, KT, T], F32R)
        ml = sb("mix_low", [P, KT, T], F32R)
        cst = sb("constants_sb", [P, C_END])
        gn = sb("gains_sb", [P, NG])
        small = sb("small", [P, 96])
        ARENA = 17100
        arena = sb("arena", [P, ARENA])
        x = arena[:, 0:KT * T].rearrange("p (k t) -> p k t", t=T)
        used = [0]

        def take(*shape):
            n = int(np.prod(shape))
            ap = arena[:, used[0]:used[0] + n]
            used[0] += n
            assert used[0] <= ARENA, used[0]
            if len(shape) == 2:
                ap = ap.rearrange("p (a b) -> p a b", b=shape[1])
            if len(shape) == 3:
                ap = ap.rearrange("p (a b c) -> p a b c", b=shape[1], c=shape[2])
            return ap

        def flat(ap):
            return ap.rearrange("p a b -> p (a b)")

        def bc(ap, n):
            return ap.unsqueeze(1).broadcast_to([P, n, ap.shape[1]])

        r3 = take(3, T + 1)
        d3 = take(3, T)
        xm = take(3, T)
        lw = take(T)
        ag = take(T)
        b_sum = take(2, P + 1)
        e1 = take(2, P + 1)
        e2 = take(2, P)
        AR = take(2, 2, P)
        bk = take(2, T)
        rkb = take(T)
        Vn = take(2, P)
        LTR = take(4, 2 * P)
        KTR = take(4, 2 * P)
        TT = take(4, 2, P)
        Xb = take(2, 4, P)
        Zs = take(4, P)
        nR = take(2, P)
        Us = take(2, P)
        kbn = take(2, P)
        S0 = take(P)
        yc = take(4, 64)
        ysq = take(4, 64)
        yT = take(T)
        otmp = take(T)
        thw = take(T)
        sgl = take(T)
        wa = take(P)
        gu = take(P)
        pj = take(NPAR)
        pln = take(2)
        aqk = take(2, T)
        av = take(T)
        aro = take(2, T)
        qk = take(2, T)
        prob = take(2, 3 * P)
        wq = take(3 * P)
        wt = take(3 * P)
        avn = take(2, P)
        on = take(2, P)
        atmp = take(T)

        used[0] = KT * T
        hf, hi, hg, hq = take(T), take(T), take(T), take(T)
        fs = take(T)
        gs = take(T)
        lf = take(T)
        hb = take(T)
        hk = take(T)
        DD = take(8, T)
        XX = take(8, T)
        AM = take(8, T)
        A01 = take(P)
        In = take(2, P)
        hon = take(2, P)
        htmp = take(T)
        hpar = take(2)
        used[0] = KT * T
        sil = take(2, T)
        hid32 = take(2, T)
        nsq = take(4, T)
        nss = take(T)
        nrs = take(T)
        n32 = take(2, T)
        lamv = take(2, 64)

        ident = cst[:, C_ID:C_ID + P]
        ones = cst[:, C_ONES:C_ONES + P]
        head_ones = cst[:, C_HEAD:C_HEAD + P]
        rot = cst[:, C_ROT:C_ROT + P]

        def level_mask(l):
            return cst[:, C_LVL + l * P:C_LVL + (l + 1) * P]

        c_eps, c_gn, c_ln08, c_shift = (small[:, i:i + 1] for i in range(4))
        nlam = small[:, 7:8]
        lamt = small[:, 8:12]
        omka = small[:, 12:13]
        nbm = small[:, 13:15]
        pbm = small[:, 15:17]
        ebm = small[:, 17:18]
        scl = small[:, 18:19]
        ymean = small[:, 20:24]
        yvar = small[:, 24:28]
        yrs = small[:, 32:36]
        amx = small[:, 36:40]
        anb = small[:, 40:44]
        asum = small[:, 44:48]
        ass = small[:, 52:54]
        aln = small[:, 54:56]
        ars = small[:, 56:58]
        hlb = small[:, 60:76]
        homl = small[:, 76:92]

        acc = [ctx.enter_context(nc.psum_tensor(f"acc{i}", [P, 512], F32)) for i in range(2)]
        pm = ctx.enter_context(nc.psum_tensor("mixer_banks", [P, 6 * 512], F32))

        def bank(b, n=1):
            return pm[:, b * 512:(b + n) * 512]

        landed = [sem(f"w_landed{i}") for i in range(RAW)]
        high_done = sem("w_high_done")
        low_done = sem("w_low_done")
        half_done = sem("half_products_done")
        evac_done = sem("product_evacuated")
        S = {}
        for group in (
            "consts_in x_in x_back credits sq sq_sum sq_total norm_ln norm_rstd h32 h_high h_low out_done",
            "lam_vec lam_sum lam_exp lb_diff lb one_minus_lb",
            "low_zero low_diff low_mixed low_acts",
            "hid_high hid_done",
            "rw_par rw_late rw_d rw_xr rw_xk rw_xv rw_za rw_sig rw_a rw_lw rw_b rw_mid rw_e1 rw_e2 rw_ebm rw_scl rw_omka rw_sq rw_kk",
            "rw_ss rw_ssmax rw_ssln rw_rn rw_kkn rw_t1 rw_k2 rw_at rw_kka rw_bt rw_kt rw_rt rw_rk rw_bonus rw_bv rw_vt rw_vn",
            "rw_m1 rw_m2 rw_m3 rw_LTR rw_KTR rw_T0 rw_TT rw_X rw_Z rw_Zs rw_TXT rw_kbT rw_kbn rw_R0 rw_nR0 rw_U0 rw_Us0",
            "rw_S rw_S0 rw_R1 rw_nR1 rw_U1 rw_Us1 rw_y rw_ymean rw_yc rw_ysq rw_yvar rw_yln rw_yrs rw_yn rw_yT rw_yTs",
            "rw_sum rw_g rw_out rw_hi rw_end",
            "at_rot at_sin at_cos at_qk at_s at_sm at_mx at_nb at_p at_rc at_w0 at_w at_wT at_wt at_vT at_vn at_o at_ss at_ln",
            "at_rs at_on at_oT at_out at_hi at_end",
            "hg_par hg_fs hg_gs hg_silu hg_lf hg_k hg_b hg_D hg_E hg_X hg_mm hg_AM hg_AT hg_A01 hg_iT hg_In hg_o hg_ss",
            "hg_ln hg_rs hg_on hg_oT hg_out hg_hi hg_end",
        ):
            for name in group.split():
                S[name] = sem(name)

        def waits(eng, count, *names):
            for name in names:
                eng.wait_ge(S[name], count)

        class Block:

            def __init__(self, base, i=None, step=0, kt=KT):
                self.kt = kt
                self.n = base if i is None else base + step * i
                self.loads = base // RAW + 1 if i is None else base // RAW + 1 + step // RAW * i
                self.raw, self.res, self.acc = base % RAW, base % RES, base % 2

            def load(self, sp, src):
                sp.wait_ge(low_done, 2 * self.n + 2)
                sp.dma_start(raw[:, self.raw, 0:self.kt], src).then_inc(landed[self.raw], 16)

            def high(self, act, half):
                ks = slice(half * HALF, half * HALF + HALF)
                act.wait_ge(landed[self.raw], self.loads * 16)
                act.wait_ge(half_done, 2 * self.n + half + 1)
                act.activation(wh[:, self.res, ks], raw[:, self.raw, ks], ACT.Copy).then_inc(high_done, 1)

            def low(self, dve, half):
                ks = slice(half * HALF, half * HALF + HALF)
                dve.wait_ge(high_done, 2 * self.n + half + 1)
                dve.tensor_tensor(wl[:, self.res, ks], raw[:, self.raw, ks],
                                  wh[:, self.res, ks].bitcast(F32), ALU.subtract).then_inc(low_done, 1)

            def products(self, pe, half, high, low):
                pe.wait_ge(low_done, 2 * self.n + half + 1 + 2 * RAW)
                if half == 0:
                    pe.wait_ge(evac_done, self.n + 1)
                o = acc[self.acc][:, 0:T]
                for k in range(half * HALF, min(self.kt, half * HALF + HALF)):
                    pe.matmul(o, wh[:, self.res, k], high[:, k], start=k == 0, stop=False)
                    pe.matmul(o, wh[:, self.res, k], low[:, k], start=False, stop=False)
                    last = pe.matmul(o, wl[:, self.res, k], high[:, k], start=False, stop=k == self.kt - 1)
                last.then_inc(half_done, 1)

            def result(self, eng):
                eng.wait_ge(half_done, 2 * self.n + 2 + 2 * RES)
                return acc[self.acc][:, 0:T]

            def wait_evacuated(self, eng):
                eng.wait_ge(evac_done, self.n + 1 + 2)

        LOWRANK = 0
        EVEN = 2
        EVEN_OUT = EVEN + 6 * NRW
        FFN = []
        n = EVEN_OUT + KT
        for layer in range(2):
            at = []
            for m in PASSES:
                at.append((n, n + 2 * m))
                n += 2 * m + KT
            FFN.append(at)
            if layer == 0:
                ODD = n
                ODD_OUT = ODD + 4 * NHG
                n = ODD_OUT + KT

        TOTAL = n
        NORM_AT = [0, FFN[0][0][0], ODD, FFN[1][0][0], TOTAL]

        def evacuated(eng, n):
            eng.wait_ge(evac_done, n + 1 + 2)

        block = ctx.enter_context(nc.Block())

        @block.sync
        def _(sp):
            sp.dma_start(cst[:], consts).then_inc(S["consts_in"], 16)
            sp.dma_start(gn[:], gains).then_inc(S["consts_in"], 16)
            sp.dma_start(x, xT).then_inc(S["x_in"], 16)
            for n in range(LOWRANK, EVEN + 6):
                Block(n).load(sp, w_even[n])
            with sp.Fori(0, 3) as i:
                for u in range(12):
                    Block(EVEN + 6 + u, i, 12).load(sp, w_even[EVEN + 6 + u + 12 * i])
            for n in range(EVEN + 42, EVEN + 48):
                Block(n).load(sp, w_even[n])

            def square(base, w):
                with sp.Fori(0, KT // 4) as i:
                    for u in range(4):
                        Block(base + u, i, 4).load(sp, w[u + 4 * i])

            def ffn(layer):
                first = 0
                for m, (gate_up, down) in zip(PASSES, FFN[layer]):
                    with sp.Fori(0, m // 2) as i:
                        for u in range(4):
                            Block(gate_up + u, i, 4).load(sp, w_gu[layer][2 * first + u + 4 * i])
                    with sp.Fori(0, KT // 4) as i:
                        for u in range(4):
                            Block(down + u, i, 4, kt=m).load(sp, w_down[layer][u + 4 * i][:, first:first + m])
                    first += m

            square(EVEN_OUT, w_even_out)
            ffn(0)
            with sp.Fori(0, NHG) as i:
                for u in range(4):
                    Block(ODD + u, i, 4).load(sp, w_odd[u + 4 * i])
            square(ODD_OUT, w_odd_out)
            ffn(1)
            sp.wait_ge(S["h32"], 5 * KT)
            sp.dma_start(out, x).then_inc(S["out_done"], 16)
            sp.wait_ge(S["out_done"], 16)

        @block.gpsimd
        def _(pool):
            def even_step(j):
                evacuated(pool, EVEN + 6 * j + 4)
                pool.wait_ge(S["at_end"], j + 1)
                for c in range(2):
                    pool.tensor_tensor(qk[:, c], aqk[:, c], cst[:, C_COS:C_COS + T], ALU.mult).then_inc(S["at_cos"], 1)
                pool.wait_ge(S["rw_LTR"], 2 * j + 2)
                for l in range(1, LEVELS):
                    pool.wait_ge(S["rw_Z"], 6 * j + max(l - 2, 0))
                    pool.tensor_tensor(Xb[:, l % 2], LTR[:, :, 0:P], bc(level_mask(l), 4), ALU.mult).then_inc(S["rw_X"], 1)

            pool.wait_ge(S["consts_in"], 32)
            even_step(0)
            with pool.Fori(0, 3) as i:
                for e in range(2):
                    even_step(1 + 2 * i + e)
            even_step(7)
            waits(pool, NRW + 1, "rw_end", "at_end")
            pool.dma_start(x, xT).then_inc(S["x_back"], 16)

            with pool.Fori(0, NHG) as h:
                for l in range(8):
                    b = 1 << l
                    pool.wait_ge(S["hg_E"], 2 * h + 1 + l // 4)
                    if l == 0:
                        pool.wait_ge(S["hg_k"], h + 1)
                    first = [t.rearrange("p (n s b) -> p n s b", s=2, b=b)[:, :, 0] for t in (XX[:, l], DD[:, l], hk)]
                    pool.tensor_tensor(*first, ALU.mult).then_inc(S["hg_X"], 1)

        @block.scalar
        def _(act):
            def norm(m):
                for k in range(KT):
                    if k >= 4:
                        act.wait_ge(S["sq_sum"], m * KT + k - 3)
                    elif m > 0 and k == 0:
                        act.wait_ge(S["h32"], m * KT)
                    if m > 0 and k == 0:
                        act.wait_ge(evac_done, NORM_AT[m] + 2)
                    act.activation(nsq[:, k % 4], x[:, k], ACT.Square).then_inc(S["sq"], 1)
                act.wait_ge(S["sq_total"], m + 1)
                act.activation(nrs, bank(0)[:, 0:T], ACT.Ln, bias=c_eps, scale=1.0 / D).then_inc(S["norm_ln"], 1)
                act.wait_ge(S["norm_ln"], m + 1)
                act.activation(nrs, nrs, ACT.Exp, scale=-0.5).then_inc(S["norm_rstd"], 1)
                for k in range(KT if m < 4 else 0):
                    act.wait_ge(S["h32"], m * KT + k + 1)
                    act.activation(hh[:, k], n32[:, k % 2], ACT.Copy).then_inc(S["h_high"], 1)

            waits(act, 1, "credits")
            act.wait_ge(S["x_in"], 16)
            act.wait_ge(S["lam_sum"], 1)
            act.activation(lamt[:, 2:4], lamt[:, 0:2], ACT.Exp).then_inc(S["lam_exp"], 1)
            act.wait_ge(S["lb_diff"], 1)
            act.activation(hlb, homl, ACT.Sigmoid).then_inc(S["lb"], 1)
            norm(0)
            act.dma_start(wa, wa_up[0]).then_inc(S["rw_par"], 16)
            act.dma_start(pj, par[0]).then_inc(S["rw_par"], 16)
            act.dma_start(gu[0:32], g_up[0]).then_inc(S["rw_late"], 16)
            act.dma_start(pln, par_ln[0]).then_inc(S["rw_late"], 16)
            for n in range(2):
                for half in range(2):
                    Block(LOWRANK + n).high(act, half)
            for n in range(2):
                Block(LOWRANK + n + 2).high(act, 0)
                product = Block(LOWRANK + n).result(act)
                act.wait_ge(S["low_zero"], 2)
                act.activation(r3[:, n, 1:], product, ACT.Copy).then_inc(evac_done, 1)
                Block(LOWRANK + n + 2).high(act, 1)
            act.wait_ge(S["low_mixed"], 2)
            act.activation(thw[0:64], xm[0:64, 0], ACT.Tanh).then_inc(S["low_acts"], 1)
            act.activation(thw[64:128], xm[64:128, 0], ACT.Copy).then_inc(S["low_acts"], 1)
            act.activation(sgl[0:32], xm[0:32, 1], ACT.Sigmoid).then_inc(S["low_acts"], 1)
            act.wait_ge(S["low_acts"], 3)

            def feed(this, ahead, dst, wait=None):
                ahead.high(act, 0)
                product = this.result(act)
                if wait:
                    wait()
                act.activation(dst, product, ACT.Copy).then_inc(evac_done, 1)
                ahead.high(act, 1)

            even_dst = [r3[:, 0, 1:], r3[:, 1, 1:], r3[:, 2, 1:], aqk[:, 0], aqk[:, 1], av]

            def even_feed(u, blocks, j):
                if blocks is None:
                    return

                def wait():
                    if u < 3:
                        act.wait_ge(S["rw_xv"], j + 1)
                    elif u < 5:
                        act.wait_ge(S["at_rot"], j + 1)
                        act.wait_ge(S["at_cos"], 2 * j + 2)
                    else:
                        act.wait_ge(S["at_vT"], j + 1)
                feed(blocks[u], blocks[u + 2], even_dst[u], wait)

            def even_step(j, blocks):
                act.wait_ge(S["rw_za"], j + 1)
                act.activation(lw, bank(5)[:, 0:T], ACT.Sigmoid, bias=pj[:, P_W0:P_W0 + 1]).then_inc(S["rw_sig"], 1)
                act.activation(ag, bank(0)[:, 0:T], ACT.Sigmoid, bias=pj[:, P_A0:P_A0 + 1]).then_inc(S["rw_a"], 1)
                act.wait_ge(S["rw_xv"], j + 1)
                act.activation(d3[:, 2], xm[:, 1], ACT.Square, scale=pj[:, P_KK:P_KK + 1]).then_inc(S["rw_sq"], 1)
                act.wait_ge(S["rw_b"], 2 * j + 2)
                act.wait_ge(S["rw_mid"], 2 * j + 2)
                for c in range(2):
                    act.activation(e1[:, c], b_sum[:, c], ACT.Exp, bias=nbm[:, c:c + 1]).then_inc(S["rw_e1"], 1)
                    act.activation(e2[:, c], b_sum[:, c, 1:], ACT.Exp, bias=pbm[:, c:c + 1], scale=-1.0).then_inc(S["rw_e2"], 1)
                act.activation(ebm, pbm[:, 1:2], ACT.Exp).then_inc(S["rw_ebm"], 1)
                act.wait_ge(S["rw_ssmax"], j + 1)
                act.activation(d3[:, 2], d3[:, 2], ACT.Ln, scale=2.0 ** LOG_SHIFT).then_inc(S["rw_ssln"], 1)
                act.wait_ge(S["rw_ssln"], j + 1)
                act.activation(d3[:, 2], d3[:, 2], ACT.Exp, scale=-0.5, bias=c_shift).then_inc(S["rw_rn"], 1)
                act.wait_ge(S["rw_vt"], j + 1)
                act.activation(flat(Vn), bank(4)[:, 256:512], ACT.Copy).then_inc(S["rw_vn"], 1)
                if blocks is not None:
                    waits(act, j + 1, "rw_rk", "rw_t1", "rw_kk", "rw_sq", "rw_a")
                    act.dma_start(wa, wa_up[j + 1]).then_inc(S["rw_par"], 16)
                    act.dma_start(pj, par[j + 1]).then_inc(S["rw_par"], 16)

                def z_copy(l):
                    act.wait_ge(S["rw_Z"], 6 * j + l)
                    act.activation(flat(Zs), bank(2), ACT.Copy).then_inc(S["rw_Zs"], 1)

                even_feed(0, blocks, j)
                z_copy(1)
                act.wait_ge(S["at_nb"], j + 1)
                for q, cols in enumerate((slice(0, P), slice(P, 3 * P))):
                    for c in range(2):
                        n = 2 * q + c
                        act.activation(prob[:, c, cols], prob[:, c, cols], ACT.Exp, bias=anb[:, n:n + 1], scale=0.125,
                                       accum_out=asum[:, n:n + 1]).then_inc(S["at_p"], 1)
                even_feed(1, blocks, j)
                z_copy(2)
                act.wait_ge(S["at_wT"], j + 1)
                act.activation(wt, bank(3)[:, 0:384], ACT.Copy).then_inc(S["at_wt"], 1)
                act.wait_ge(S["at_vT"], j + 1)
                act.activation(flat(avn), bank(4)[:, 0:256], ACT.Copy).then_inc(S["at_vn"], 1)
                even_feed(2, blocks, j)
                z_copy(3)
                act.wait_ge(S["at_o"], j + 1)
                for q in range(2):
                    act.activation(on[:, q], bank(3)[:, q * P:(q + 1) * P], ACT.Square, accum_out=ass[:, q:q + 1]).then_inc(S["at_ss"], 1)
                act.wait_ge(S["at_ss"], 2 * j + 2)
                act.activation(aln, ass, ACT.Ln, scale=1.0 / P, bias=c_eps).then_inc(S["at_ln"], 1)
                act.wait_ge(S["at_ln"], j + 1)
                act.activation(ars, aln, ACT.Exp, scale=-0.5, bias=c_ln08).then_inc(S["at_rs"], 1)
                even_feed(3, blocks, j)
                z_copy(4)
                even_feed(4, blocks, j)
                z_copy(5)
                act.wait_ge(S["rw_kbT"], j + 1)
                act.activation(flat(kbn), bank(5)[:, 0:256], ACT.Copy).then_inc(S["rw_kbn"], 1)
                z_copy(6)
                act.wait_ge(S["rw_R0"], j + 1)
                act.activation(nR[:, 0], bank(5)[:, 256:384], ACT.Copy, scale=-1.0).then_inc(S["rw_nR0"], 1)
                even_feed(5, blocks, j)
                act.wait_ge(S["rw_U0"], j + 1)
                act.activation(Us[:, 0], bank(5)[:, 384:512], ACT.Copy).then_inc(S["rw_Us0"], 1)
                act.wait_ge(S["rw_R1"], j + 1)
                act.activation(nR[:, 1], bank(1)[:, 0:P], ACT.Copy, scale=-1.0).then_inc(S["rw_nR1"], 1)
                act.wait_ge(S["rw_U1"], j + 1)
                act.activation(Us[:, 1], bank(2)[:, 0:P], ACT.Copy).then_inc(S["rw_Us1"], 1)
                act.wait_ge(S["rw_yc"], j + 1)
                act.activation(ysq, yc, ACT.Square).then_inc(S["rw_ysq"], 1)
                act.wait_ge(S["rw_yvar"], j + 1)
                act.activation(yrs, yvar, ACT.Ln, scale=1.0 / 64, bias=c_gn).then_inc(S["rw_yln"], 1)
                act.wait_ge(S["rw_yln"], j + 1)
                act.activation(yrs, yrs, ACT.Exp, scale=-0.5).then_inc(S["rw_yrs"], 1)
                act.wait_ge(S["rw_yT"], j + 1)
                act.wait_ge(S["rw_late"], 32 * j + 32)
                act.activation(yT, bank(1)[:, 256:512], ACT.Identity, scale=pln[:, 0:1], bias=pln[:, 1:2]).then_inc(S["rw_yTs"], 1)
                if blocks is not None:
                    waits(act, j + 1, "rw_yTs", "rw_g")
                    act.dma_start(gu[0:32], g_up[j + 1]).then_inc(S["rw_late"], 16)
                    act.dma_start(pln, par_ln[j + 1]).then_inc(S["rw_late"], 16)

            for u in range(6):
                feed(Block(EVEN + u), Block(EVEN + u + 2), even_dst[u])
            even_step(0, [Block(EVEN + 6 + u) for u in range(8)])
            with act.Fori(0, 3) as i:
                for e in range(2):
                    even_step(1 + 2 * i + e, [Block(EVEN + 12 + 6 * e + u, i, 12) for u in range(8)])
            even_step(7, None)

            def square(base):
                at_end = base + KT == TOTAL
                with act.Fori(0, KT // 4 - at_end) as i:
                    for u in range(4):
                        for half in range(2):
                            Block(base + 2 + u, i, 4).high(act, half)
                if at_end:
                    for n in range(TOTAL - 2, TOTAL):
                        for half in range(2):
                            Block(n).high(act, half)

            def ffn(layer):
                norm(1 + 2 * layer)
                first = 0
                for m, (gate_up, down) in zip(PASSES, FFN[layer]):
                    with act.Fori(0, m // 2) as i:
                        for b in range(2):
                            gate = Block(gate_up + 2 * b, i, 4)
                            Block(gate_up + 2 * b + 2, i, 4).high(act, 0)
                            product = gate.result(act)
                            act.wait_ge(evac_done, gate.n + 2)
                            act.activation(sil[:, b], product, ACT.Silu).then_inc(evac_done, 1)
                            Block(gate_up + 2 * b + 2, i, 4).high(act, 1)
                            for half in range(2):
                                Block(gate_up + 2 * b + 3, i, 4).high(act, half)
                    square(down)
                    first += m

            square(EVEN_OUT)
            ffn(0)
            norm(2)
            head_dst = [hf, hi, hg, hq]

            def odd_step(h, blocks):
                evacuated(act, ODD + 4 * h + 2)
                act.activation(fs, hf, ACT.Sigmoid).then_inc(S["hg_fs"], 1)
                act.wait_ge(S["hg_end"], h + 1)
                act.activation(gs, hg, ACT.Sigmoid).then_inc(S["hg_gs"], 1)
                act.wait_ge(S["hg_par"], 2 * h + 2)
                act.wait_ge(S["hg_fs"], h + 1)
                act.activation(lf, fs, ACT.Ln, scale=hpar[:, 1:2], bias=hpar[:, 0:1]).then_inc(S["hg_lf"], 1)
                act.wait_ge(S["hg_iT"], h + 1)
                act.activation(flat(In), bank(5)[:, 0:256], ACT.Copy).then_inc(S["hg_In"], 1)
                for half in range(2):
                    if half and blocks:
                        blocks[2].high(act, 0)
                    act.wait_ge(S["hg_D"], 16 * h + 8 * half + 8)
                    part = DD[:, 4 * half:4 * half + 4]
                    act.activation(part, part, ACT.Exp).then_inc(S["hg_E"], 1)
                if blocks:
                    act.activation(head_dst[0], blocks[0].result(act), ACT.Copy).then_inc(evac_done, 1)
                    blocks[2].high(act, 1)
                    feed(blocks[1], blocks[3], head_dst[1])
                    act.wait_ge(S["hg_silu"], h + 1)
                    feed(blocks[2], blocks[4], head_dst[2])
                act.wait_ge(S["hg_o"], h + 1)
                for q in range(2):
                    act.activation(hon[:, q], bank(5)[:, 256 + q * P:256 + (q + 1) * P], ACT.Square,
                                   accum_out=ass[:, q:q + 1]).then_inc(S["hg_ss"], 1)
                act.wait_ge(S["hg_ss"], 2 * h + 2)
                act.activation(aln, ass, ACT.Ln, scale=1.0 / P, bias=c_eps).then_inc(S["hg_ln"], 1)
                act.wait_ge(S["hg_ln"], h + 1)
                act.activation(ars, aln, ACT.Exp, scale=-0.5).then_inc(S["hg_rs"], 1)
                if blocks:
                    feed(blocks[3], blocks[5], head_dst[3])

            for u in range(4):
                feed(Block(ODD + u), Block(ODD + u + 2), head_dst[u])
            with act.Fori(0, NHG - 1) as h:
                odd_step(h, [Block(ODD + 4 + u, h, 4) for u in range(6)])
            odd_step(NHG - 1, None)
            square(ODD_OUT)
            ffn(1)
            norm(4)

        @block.vector
        def _(dve):
            def norm(m, gain):
                for k in range(KT):
                    dve.wait_ge(S["sq"], m * KT + k + 1)
                    if k == 0:
                        dve.tensor_copy(nss, nsq[:, 0]).then_inc(S["sq_sum"], 1)
                    else:
                        dve.wait_ge(S["sq_sum"], m * KT + k)
                        dve.tensor_tensor(nss, nss, nsq[:, k % 4], ALU.add).then_inc(S["sq_sum"], 1)
                dve.wait_ge(S["norm_rstd"], m + 1)
                for k in range(KT):
                    g = gn[:, gain + k:gain + k + 1]
                    if m == 4:
                        dve.scalar_tensor_tensor(x[:, k], x[:, k], g, nrs, ALU.mult, ALU.mult).then_inc(S["h32"], 1)
                        continue
                    if k >= 2:
                        dve.wait_ge(S["h_low"], m * KT + k - 1)
                    dve.scalar_tensor_tensor(n32[:, k % 2], x[:, k], g, nrs, ALU.mult, ALU.mult).then_inc(S["h32"], 1)
                    for kk in ([k - 1] if k else []) + ([k] if k == KT - 1 else []):
                        dve.wait_ge(S["h_high"], m * KT + kk + 1)
                        dve.tensor_tensor(hl[:, kk], n32[:, kk % 2], hh[:, kk].bitcast(F32), ALU.subtract).then_inc(S["h_low"], 1)

            dve.sem_inc(low_done, 2 * RAW)
            for name in ("rw_end", "at_end", "hg_end"):
                dve.sem_inc(S[name], 1)
            dve.memset(c_eps, EPS)
            dve.memset(c_gn, GN_EPS)
            dve.memset(c_ln08, math.log(1.0 - LAM_INIT))
            dve.memset(c_shift, LOG_SHIFT / 2 * math.log(2.0)).then_inc(S["credits"], 1)
            dve.wait_ge(S["consts_in"], 32)
            dve.tensor_tensor(homl, gn[:, G_LB1:G_LB1 + 16], gn[:, G_LB0:G_LB0 + 16], ALU.subtract).then_inc(S["lb_diff"], 1)
            l4 = gn[:, G_LAM:G_LAM + 256].rearrange("p (a b c) -> p a b c", a=2, b=2)
            dve.tensor_tensor(lamv, l4[:, :, 0], l4[:, :, 1], ALU.mult).then_inc(S["lam_vec"], 1)
            dve.wait_ge(S["lam_vec"], 1)
            dve.reduce_sum(lamt[:, 0:2], lamv, AX.X).then_inc(S["lam_sum"], 1)
            dve.wait_ge(S["lam_exp"], 1)
            dve.tensor_tensor(lamt[:, 0:1], lamt[:, 3:4], lamt[:, 2:3], ALU.subtract).then_inc(S["lam_vec"], 1)
            dve.wait_ge(S["lam_vec"], 2)
            dve.tensor_scalar(nlam, lamt[:, 0:1], -LAM_INIT, None, ALU.add).then_inc(S["lam_vec"], 1)
            dve.wait_ge(S["lb"], 1)
            dve.tensor_scalar(homl, hlb, -1.0, 1.0, ALU.mult, ALU.add).then_inc(S["one_minus_lb"], 1)
            dve.wait_ge(S["lam_vec"], 3)
            dve.wait_ge(S["one_minus_lb"], 1)
            norm(0, G_ATT0)
            dve.wait_ge(S["h_low"], KT)
            dve.memset(r3[:, :, 0:1], 0.0).then_inc(S["low_zero"], 1)
            dve.memset(b_sum[:, :, 0:1], 0.0).then_inc(S["low_zero"], 1)
            for n in range(2):
                for half in range(2):
                    Block(LOWRANK + n).low(dve, half)
            for n in range(2):
                Block(LOWRANK + n + 2).low(dve, 0)
                Block(LOWRANK + n).wait_evacuated(dve)
                dve.tensor_tensor(d3[:, n], r3[:, n, 0:T], r3[:, n, 1:], ALU.subtract).then_inc(S["low_diff"], 1)
                dve.wait_ge(S["low_diff"], n + 1)
                dve.scalar_tensor_tensor(xm[:, n], d3[:, n], gn[:, G_MUW + n:G_MUW + n + 1], r3[:, n, 1:],
                                         ALU.mult, ALU.add).then_inc(S["low_mixed"], 1)
                Block(LOWRANK + n + 2).low(dve, 1)

            def even_step(j, blocks):
                def low(u):
                    if blocks is not None:
                        for half in range(2):
                            blocks[u + 2].low(dve, half)

                evacuated(dve, EVEN + 6 * j + 2)
                dve.wait_ge(S["rw_end"], j + 1)
                dve.wait_ge(S["rw_par"], 32 * j + 32)
                dve.tensor_tensor(d3, r3[:, :, 0:T], r3[:, :, 1:], ALU.subtract).then_inc(S["rw_d"], 1)
                dve.tensor_scalar(omka, pj[:, P_KA:P_KA + 1], -1.0, 1.0, ALU.mult, ALU.add).then_inc(S["rw_omka"], 1)
                dve.wait_ge(S["rw_d"], j + 1)
                for c, name in ((1, "rw_xk"), (0, "rw_xr"), (2, "rw_xv")):
                    dve.scalar_tensor_tensor(xm[:, c], d3[:, c], pj[:, P_MU + c:P_MU + c + 1], r3[:, c, 1:],
                                             ALU.mult, ALU.add).then_inc(S[name], 1)
                dve.wait_ge(S["rw_sig"], j + 1)
                dve.tensor_scalar(lw, lw, NEG_EXP_HALF, None, ALU.mult).then_inc(S["rw_lw"], 1)
                waits(dve, j + 1, "rw_xk", "rw_xr", "rw_xv")
                dve.tensor_scalar(d3[:, 1], xm[:, 1], pj[:, P_KK:P_KK + 1], None, ALU.mult).then_inc(S["rw_kk"], 1)
                dve.wait_ge(S["rw_lw"], j + 1)
                for c in range(2):
                    dve.tensor_tensor_scan(b_sum[:, c, 1:], ones, lw[:, c * P:(c + 1) * P], 0.0, ALU.mult, ALU.add).then_inc(S["rw_b"], 1)
                dve.wait_ge(S["rw_b"], 2 * j + 2)
                mid = b_sum[:, :, P // 2]
                dve.tensor_scalar(nbm, mid, -1.0, None, ALU.mult).then_inc(S["rw_mid"], 1)
                dve.tensor_scalar(pbm, mid, 1.0, None, ALU.mult).then_inc(S["rw_mid"], 1)
                waits(dve, j + 1, "rw_ss", "rw_sq")
                dve.tensor_scalar(d3[:, 2], bank(2)[:, 0:T], 1e-24, None, ALU.max).then_inc(S["rw_ssmax"], 1)
                waits(dve, j + 1, "rw_a", "rw_omka")
                dve.tensor_scalar(d3[:, 0], ag, pj[:, P_KA:P_KA + 1], omka, ALU.mult, ALU.add).then_inc(S["rw_t1"], 1)
                dve.wait_ge(S["rw_t1"], j + 1)
                dve.tensor_tensor(d3[:, 0], d3[:, 0], xm[:, 1], ALU.mult).then_inc(S["rw_k2"], 1)
                dve.wait_ge(S["rw_k2"], j + 1)
                dve.scalar_tensor_tensor(rkb, xm[:, 0], pj[:, P_RK:P_RK + 1], d3[:, 0], ALU.mult, ALU.mult).then_inc(S["rw_rk"], 1)
                dve.wait_ge(S["rw_e2"], 2 * j + 2)
                dve.tensor_tensor(bk[:, 1], d3[:, 0], flat(e2), ALU.mult).then_inc(S["rw_kt"], 1)
                dve.wait_ge(S["rw_e1"], 2 * j + 2)
                dve.tensor_tensor(AR[:, :, 1], xm[:, 0].rearrange("p (c t) -> p c t", c=2), e1[:, :, 1:], ALU.mult).then_inc(S["rw_rt"], 1)
                waits(dve, j + 1, "rw_rn", "rw_kk")
                dve.tensor_tensor(d3[:, 1], d3[:, 1], d3[:, 2], ALU.mult).then_inc(S["rw_kkn"], 1)
                dve.wait_ge(S["rw_kkn"], j + 1)
                dve.tensor_tensor(AR[:, :, 0], d3[:, 1].rearrange("p (c t) -> p c t", c=2), e1[:, :, 0:P], ALU.mult).then_inc(S["rw_at"], 1)
                dve.tensor_tensor(d3[:, 2], d3[:, 1], ag, ALU.mult).then_inc(S["rw_kka"], 1)
                dve.wait_ge(S["rw_kka"], j + 1)
                dve.tensor_tensor(bk[:, 0], d3[:, 2], flat(e2), ALU.mult).then_inc(S["rw_bt"], 1)
                dve.wait_ge(S["rw_ebm"], j + 1)
                dve.tensor_tensor(scl, ebm, e1[:, 0, P:P + 1], ALU.mult).then_inc(S["rw_scl"], 1)
                dve.wait_ge(S["at_rot"], j + 1)
                dve.tensor_tensor(aro, bank(3).rearrange("p (a b) -> p a b", a=2), bc(cst[:, C_SIN:C_SIN + T], 2), ALU.mult).then_inc(S["at_sin"], 1)
                dve.wait_ge(S["at_sin"], j + 1)
                dve.wait_ge(S["at_cos"], 2 * j + 2)
                dve.tensor_tensor(qk, qk, aro, ALU.add).then_inc(S["at_qk"], 1)
                low(0)
                tri = bc(cst[:, C_TRI:C_TRI + 2 * P], 2)
                dve.wait_ge(S["rw_m1"], j + 1)
                for n in range(2):
                    dve.tensor_tensor(LTR[:, 2 * n:2 * n + 2], bank(n).rearrange("p (a b) -> p a b", a=2), tri, ALU.mult).then_inc(S["rw_LTR"], 1)
                dve.wait_ge(S["rw_m3"], j + 1)
                for h in range(2):
                    dve.tensor_tensor(TT[:, 2 * h:2 * h + 2, 0], bank(5 - h)[:, 0:T].rearrange("p (a b) -> p a b", a=2),
                                      bc(cst[:, C_LOW0:C_LOW0 + P], 2), ALU.mult).then_inc(S["rw_T0"], 1)
                dve.wait_ge(S["rw_LTR"], 2 * j + 2)
                dve.tensor_tensor(TT[:, :, 1], LTR[:, :, 0:P], bc(level_mask(0), 4), ALU.mult).then_inc(S["rw_T0"], 1)
                dve.wait_ge(S["rw_T0"], 3 * j + 3)
                t8 = TT.rearrange("p a b c -> p (a b) c")
                dve.tensor_tensor(t8, bc(ident, 8), t8, ALU.subtract).then_inc(S["rw_TT"], 1)
                dve.wait_ge(S["rw_m2"], j + 1)
                for n in range(2):
                    dve.tensor_tensor(KTR[:, 2 * n:2 * n + 2], bank(2 + n).rearrange("p (a b) -> p a b", a=2), tri, ALU.mult).then_inc(S["rw_KTR"], 1)

                def level(l):
                    dve.wait_ge(S["rw_TXT"], 6 * j + l)
                    if l < LEVELS - 1:
                        t = TT.rearrange("p a b c -> p (a b c)")
                        dve.tensor_tensor(t, t, bank(0, 2), ALU.subtract).then_inc(S["rw_TT"], 1)
                    else:
                        t = TT[:, :, 1]
                        dve.tensor_tensor(t, t, bank(0, 2).rearrange("p (a b c) -> p a b c", a=4, b=2)[:, :, 1], ALU.subtract).then_inc(S["rw_TT"], 1)

                dve.wait_ge(S["at_s"], j + 1)
                for c in range(2):
                    dve.tensor_tensor(prob[:, c], bank(4 + c)[:, 0:384], cst[:, C_CAUSAL:C_END], ALU.add).then_inc(S["at_sm"], 1)
                dve.wait_ge(S["at_sm"], 2 * j + 2)
                dve.reduce_max(amx[:, 0:2], prob[:, :, 0:P], AX.X).then_inc(S["at_mx"], 1)
                dve.reduce_max(amx[:, 2:4], prob[:, :, P:3 * P], AX.X).then_inc(S["at_mx"], 1)
                dve.wait_ge(S["at_mx"], 2 * j + 2)
                dve.tensor_scalar(anb, amx, -0.125, None, ALU.mult).then_inc(S["at_nb"], 1)
                level(1)
                low(1)
                dve.wait_ge(S["at_p"], 4 * j + 4)
                dve.reciprocal(asum, asum).then_inc(S["at_rc"], 1)
                dve.wait_ge(S["at_rc"], 2 * j + 1)
                second = asum.rearrange("p (q c) -> p q c", c=2)[:, :, 1]
                dve.tensor_scalar(second, second, nlam, None, ALU.mult).then_inc(S["at_rc"], 1)
                dve.wait_ge(S["at_rc"], 2 * j + 2)
                for q, cols in ((0, slice(0, P)), (1, slice(P, 3 * P))):
                    dve.tensor_scalar(wq[:, cols], prob[:, 1, cols], asum[:, 2 * q + 1:2 * q + 2], None, ALU.mult).then_inc(S["at_w0"], 1)
                dve.wait_ge(S["at_w0"], 2 * j + 2)
                for q, cols in ((0, slice(0, P)), (1, slice(P, 3 * P))):
                    dve.scalar_tensor_tensor(wq[:, cols], prob[:, 0, cols], asum[:, 2 * q:2 * q + 1], wq[:, cols], ALU.mult, ALU.add).then_inc(S["at_w"], 1)
                level(2)
                low(2)
                level(3)
                dve.wait_ge(S["at_rs"], j + 1)
                dve.tensor_tensor(on, bank(3)[:, 0:256].rearrange("p (a b) -> p a b", a=2),
                                  ars.unsqueeze(2).broadcast_to([P, 2, P]), ALU.mult).then_inc(S["at_on"], 1)
                low(3)
                level(4)
                dve.wait_ge(S["at_oT"], j + 1)
                dve.tensor_scalar(atmp, bank(4)[:, 0:256], gn[:, G_SUB:G_SUB + 1], None, ALU.mult).then_inc(S["at_out"], 1)
                dve.wait_ge(S["at_out"], j + 1)
                dve.tensor_scalar(mh[:, j], atmp, 1.0, None, ALU.mult).then_inc(S["at_hi"], 1)
                dve.wait_ge(S["at_hi"], j + 1)
                dve.tensor_tensor(ml[:, j], atmp, mh[:, j].bitcast(F32), ALU.subtract).then_inc(S["at_end"], 1)
                low(4)
                level(5)
                level(6)
                low(5)
                waits(dve, j + 1, "rw_S", "rw_scl")
                dve.scalar_tensor_tensor(S0, bank(1)[:, P:2 * P], scl, head_ones, ALU.mult, ALU.mult).then_inc(S["rw_S0"], 1)
                dve.wait_ge(S["rw_y"], j + 1)
                y4 = bank(2)[:, 256:512].rearrange("p (a b) -> p a b", a=4)
                dve.reduce_sum(ymean, y4, AX.X).then_inc(S["rw_ymean"], 1)
                dve.wait_ge(S["rw_ymean"], 2 * j + 1)
                dve.tensor_scalar(ymean, ymean, 1.0 / 64, None, ALU.mult).then_inc(S["rw_ymean"], 1)
                dve.wait_ge(S["rw_ymean"], 2 * j + 2)
                dve.tensor_tensor(yc, y4, ymean.unsqueeze(2).broadcast_to([P, 4, 64]), ALU.subtract).then_inc(S["rw_yc"], 1)
                dve.wait_ge(S["rw_bonus"], j + 1)
                dve.tensor_tensor(rkb, bank(0)[:, 0:T], xm[:, 2], ALU.mult).then_inc(S["rw_bv"], 1)
                dve.wait_ge(S["rw_ysq"], j + 1)
                dve.reduce_sum(yvar, ysq, AX.X).then_inc(S["rw_yvar"], 1)
                waits(dve, j + 1, "rw_yrs", "rw_yc")
                dve.tensor_tensor(yc, yc, yrs.unsqueeze(2).broadcast_to([P, 4, 64]), ALU.mult).then_inc(S["rw_yn"], 1)
                waits(dve, j + 1, "rw_yTs", "rw_bv")
                dve.tensor_tensor(yT, yT, rkb, ALU.add).then_inc(S["rw_sum"], 1)
                waits(dve, j + 1, "rw_sum", "rw_g")
                dve.tensor_tensor(otmp, yT, bank(5)[:, 0:T], ALU.mult).then_inc(S["rw_out"], 1)
                dve.wait_ge(S["rw_out"], j + 1)
                dve.tensor_scalar(mh[:, NRW + j], otmp, 1.0, None, ALU.mult).then_inc(S["rw_hi"], 1)
                dve.wait_ge(S["rw_hi"], j + 1)
                dve.tensor_tensor(ml[:, NRW + j], otmp, mh[:, NRW + j].bitcast(F32), ALU.subtract).then_inc(S["rw_end"], 1)

            for u in range(6):
                for half in range(2):
                    Block(EVEN + u + 2).low(dve, half)
            even_step(0, [Block(EVEN + 6 + u) for u in range(8)])
            with dve.Fori(0, 3) as i:
                for e in range(2):
                    even_step(1 + 2 * i + e, [Block(EVEN + 12 + 6 * e + u, i, 12) for u in range(8)])
            even_step(7, None)

            def square(base, kt=KT):
                def one(k, this, ahead):
                    if ahead is not None:
                        ahead.low(dve, 0)
                    product = this.result(dve)
                    dve.tensor_tensor(x[:, k], x[:, k], product, ALU.add).then_inc(evac_done, 1)
                    if ahead is not None:
                        ahead.low(dve, 1)

                at_end = base + KT == TOTAL
                with dve.Fori(0, KT // 4 - at_end) as i:
                    for u in range(4):
                        one(4 * i + u, Block(base + u, i, 4, kt=kt), Block(base + 2 + u, i, 4))
                for n in range(TOTAL - 4, TOTAL if at_end else 0):
                    one(n - base, Block(n, kt=kt), Block(n + 2) if n + 2 < TOTAL else None)

            def ffn(layer, gain):
                dve.wait_ge(evac_done, FFN[layer][0][0] + 2)
                norm(1 + 2 * layer, gain)
                first = FB * layer
                for m, (gate_up, down) in zip(PASSES, FFN[layer]):
                    with dve.Fori(0, m // 2) as i:
                        for b in range(2):
                            n = first + 2 * i + b
                            up = Block(gate_up + 2 * b + 1, i, 4)
                            for half in range(2):
                                Block(gate_up + 2 * b + 2, i, 4).low(dve, half)
                            Block(gate_up + 2 * b + 3, i, 4).low(dve, 0)
                            product = up.result(dve)
                            dve.wait_ge(evac_done, up.n + 2)
                            dve.tensor_tensor(hid32[:, b], sil[:, b], product, ALU.mult).then_inc(evac_done, 1)
                            up.wait_evacuated(dve)
                            dve.tensor_scalar(mh[:, 2 * i + b], hid32[:, b], 1.0, None, ALU.mult).then_inc(S["hid_high"], 1)
                            dve.wait_ge(S["hid_high"], n + 1)
                            dve.tensor_tensor(ml[:, 2 * i + b], hid32[:, b], mh[:, 2 * i + b].bitcast(F32), ALU.subtract).then_inc(S["hid_done"], 1)
                            Block(gate_up + 2 * b + 3, i, 4).low(dve, 1)
                    square(down, kt=m)
                    first += m

            dve.wait_ge(S["x_back"], 16)
            square(EVEN_OUT)
            ffn(0, G_FFN0)
            dve.wait_ge(evac_done, ODD + 2)
            norm(2, G_ATT1)

            def odd_step(h, blocks):
                def low(u, half):
                    if blocks is not None:
                        blocks[u + 2].low(dve, half)

                evacuated(dve, ODD + 4 * h + 3)
                dve.wait_ge(S["hg_end"], h + 1)
                dve.tensor_scalar(hpar[:, 0:1], hlb[:, bass.ds(h, 1)], 1.0, None, ALU.mult).then_inc(S["hg_par"], 1)
                dve.tensor_scalar(hpar[:, 1:2], homl[:, bass.ds(h, 1)], 1.0, None, ALU.mult).then_inc(S["hg_par"], 1)
                dve.wait_ge(S["hg_par"], 2 * h + 2)
                dve.wait_ge(S["hg_gs"], h + 1)
                dve.tensor_tensor(gs, gs, hg, ALU.mult).then_inc(S["hg_silu"], 1)
                dve.wait_ge(S["hg_lf"], h + 1)
                for c in range(2):
                    dve.tensor_tensor_scan(hb[:, c * P:(c + 1) * P], ones, lf[:, c * P:(c + 1) * P], 0.0, ALU.mult, ALU.add).then_inc(S["hg_b"], 1)
                dve.scalar_tensor_tensor(hk, fs, hpar[:, 1:2], hpar[:, 1:2].broadcast_to([P, T]), ALU.mult, ALU.subtract,
                                         reverse1=True).then_inc(S["hg_k"], 1)
                dve.wait_ge(S["hg_b"], 2 * h + 2)
                for l in range(8):
                    b = 1 << l
                    hv = hb.rearrange("p (n s b) -> p n s b", s=2, b=b)
                    dv = DD[:, l].rearrange("p (n s b) -> p n s b", s=2, b=b)
                    nb = T // (2 * b)
                    ref = hv[:, :, 0, b - 1:b].broadcast_to([P, nb, b])
                    dve.tensor_tensor(dv[:, :, 0], ref, hv[:, :, 0], ALU.subtract).then_inc(S["hg_D"], 1)
                    if l < 7:
                        dve.tensor_tensor(dv[:, :, 1], hv[:, :, 1], ref, ALU.subtract).then_inc(S["hg_D"], 1)
                    else:
                        dve.tensor_scalar(dv[:, :, 1], hv[:, :, 1], 1.0, None, ALU.mult).then_inc(S["hg_D"], 1)
                    if l == 4:
                        low(0, 0)
                for l in range(8):
                    b = 1 << l
                    if l % 4 == 0:
                        dve.wait_ge(S["hg_E"], 2 * h + 1 + l // 4)
                    second = [t.rearrange("p (n s b) -> p n s b", s=2, b=b)[:, :, 1] for t in (XX[:, l], DD[:, l], hq)]
                    dve.tensor_tensor(*second, ALU.mult).then_inc(S["hg_X"], 1)
                low(0, 1)
                low(1, 0)
                low(1, 1)
                dve.wait_ge(S["hg_mm"], h + 1)
                masks = cst[:, C_LVL:C_LVL + 8 * P].rearrange("p (l t) -> p l t", t=P)
                p4 = pm[:, 0:2048].rearrange("p (l c t) -> p l c t", l=8, c=2)
                a4 = AM.rearrange("p l (c t) -> p l c t", c=2)
                for c in range(2):
                    dve.tensor_tensor(a4[:, :, c], p4[:, :, c], masks, ALU.mult).then_inc(S["hg_AM"], 1)
                dve.tensor_copy(A01, bank(4)[:, 0:P]).then_inc(S["hg_A01"], 1)
                dve.wait_ge(S["hg_AM"], 2 * h + 2)
                for n, w in enumerate((4, 2, 1)):
                    dve.tensor_tensor(AM[:, 0:w], AM[:, 0:w], AM[:, w:2 * w], ALU.add).then_inc(S["hg_AT"], 1)
                    dve.wait_ge(S["hg_AT"], 3 * h + n + 1)
                low(2, 0)
                low(2, 1)
                dve.wait_ge(S["hg_rs"], h + 1)
                dve.tensor_tensor(hon, bank(5)[:, 256:512].rearrange("p (a b) -> p a b", a=2),
                                  ars.unsqueeze(2).broadcast_to([P, 2, P]), ALU.mult).then_inc(S["hg_on"], 1)
                dve.wait_ge(S["hg_oT"], h + 1)
                dve.scalar_tensor_tensor(htmp, bank(4)[:, 256:512], gn[:, G_HGN:G_HGN + 1], gs, ALU.mult, ALU.mult).then_inc(S["hg_out"], 1)
                dve.wait_ge(S["hg_out"], h + 1)
                dve.tensor_scalar(mh[:, h], htmp, 1.0, None, ALU.mult).then_inc(S["hg_hi"], 1)
                dve.wait_ge(S["hg_hi"], h + 1)
                dve.tensor_tensor(ml[:, h], htmp, mh[:, h].bitcast(F32), ALU.subtract).then_inc(S["hg_end"], 1)
                low(3, 0)
                low(3, 1)

            for u in range(4):
                for half in range(2):
                    Block(ODD + u + 2).low(dve, half)
            with dve.Fori(0, NHG - 1) as h:
                odd_step(h, [Block(ODD + 4 + u, h, 4) for u in range(6)])
            odd_step(NHG - 1, None)
            square(ODD_OUT)
            ffn(1, G_FFN1)
            dve.wait_ge(evac_done, NORM_AT[4] + 2)
            norm(4, G_FIN)

        @block.tensor
        def _(pe):
            def norm(m):
                pe.wait_ge(S["sq_sum"], (m + 1) * KT)
                pe.matmul(bank(0)[:, 0:T], ones, nss, start=True, stop=True).then_inc(S["sq_total"], 1)
                if m < 4:
                    pe.wait_ge(S["h_low"], (m + 1) * KT)

            def transposed(out, src):
                return pe.transpose(out, src, ident)

            pe.sem_inc(half_done, 2 * RES)
            pe.sem_inc(evac_done, 2)
            pe.wait_ge(S["consts_in"], 32)
            norm(0)
            for n in range(EVEN + 6):
                for half in range(2):
                    Block(n).products(pe, half, hh, hl)

            def even_step(j, blocks):
                def dense(h):
                    if blocks is not None:
                        blocks[h // 2].products(pe, h % 2, hh, hl)

                waits(pe, j + 1, "rw_end", "at_end")
                pe.wait_ge(S["low_acts"], 3)
                pe.wait_ge(S["rw_par"], 32 * j + 32)
                pe.matmul(bank(5)[:, 0:T], wa[0:64], thw[0:64], start=True, stop=True)
                pe.matmul(bank(0)[:, 0:T], wa[64:128], thw[64:128], start=True, stop=True).then_inc(S["rw_za"], 1)
                evacuated(pe, EVEN + 6 * j + 5)
                pe.matmul(bank(3), rot, flat(aqk), start=True, stop=True).then_inc(S["at_rot"], 1)
                dense(0)
                pe.wait_ge(S["rw_sq"], j + 1)
                pe.matmul(bank(2)[:, 0:T], head_ones, d3[:, 2], start=True, stop=True).then_inc(S["rw_ss"], 1)
                pe.wait_ge(S["rw_xv"], j + 1)
                for c in range(2):
                    last = transposed(bank(4)[:, 256 + c * P:256 + (c + 1) * P], xm[:, 2, c * P:(c + 1) * P])
                last.then_inc(S["rw_vt"], 1)
                dense(1)
                waits(pe, j + 1, "rw_at", "rw_bt", "rw_rt", "rw_kt", "rw_sig", "rw_a")
                hc = [(h, c) for h in range(2) for c in range(2)]
                for n, (h, c) in enumerate(hc):
                    rows, cols = slice(64 * h, 64 * h + 64), slice(c * P, (c + 1) * P)
                    last = pe.matmul(bank(n // 2)[:, (n % 2) * 256:(n % 2) * 256 + 256], bk[rows, 0, cols],
                                     AR[rows, c].rearrange("p a b -> p (a b)"), start=True, stop=True)
                last.then_inc(S["rw_m1"], 1)
                pe.wait_ge(S["rw_vn"], j + 1)
                for n, (h, c) in enumerate(hc):
                    rows, cols = slice(64 * h, 64 * h + 64), slice(c * P, (c + 1) * P)
                    last = pe.matmul(bank(5 - h)[:, c * P:(c + 1) * P], AR[rows, c, 0], bk[rows, 0, cols], start=True, stop=True)
                last.then_inc(S["rw_m3"], 1)
                waits(pe, j + 1, "at_sin", "rw_ssmax")
                for n, (h, c) in enumerate(hc):
                    rows, cols = slice(64 * h, 64 * h + 64), slice(c * P, (c + 1) * P)
                    last = pe.matmul(bank(2 + n // 2)[:, (n % 2) * 256:(n % 2) * 256 + 256], bk[rows, 1, cols],
                                     AR[rows, c].rearrange("p a b -> p (a b)"), start=True, stop=True)
                last.then_inc(S["rw_m2"], 1)
                dense(2)
                pe.wait_ge(S["rw_T0"], 3 * j + 2)
                waits(pe, j + 1, "at_qk")
                for c in range(2):
                    rows = slice(64 * c, 64 * c + 64)
                    pe.matmul(bank(4 + c)[:, 0:P], qk[rows, 0, 0:P], qk[rows, 1, 0:P], start=True, stop=True)
                    last = pe.matmul(bank(4 + c)[:, P:3 * P], qk[rows, 0, P:T], qk[rows, 1], start=True, stop=True)
                last.then_inc(S["at_s"], 1)

                def z(l):
                    pe.wait_ge(S["rw_X"], 6 * j + l)
                    pe.wait_ge(S["rw_TT"], 7 * j + l)
                    if l == 1:
                        pe.wait_ge(S["rw_KTR"], 2 * j + 2)
                    for n in range(4):
                        last = pe.matmul(bank(2)[:, n * P:(n + 1) * P], Xb[:, l % 2, n], TT[:, n, 0], start=True, stop=True)
                    last.then_inc(S["rw_Z"], 1)

                def txt(l):
                    pe.wait_ge(S["rw_Zs"], 6 * j + l)
                    for n in range(4):
                        o = bank(0, 2)[:, n * 256:(n + 1) * 256]
                        if l < LEVELS - 1:
                            pe.matmul(o[:, 0:P], TT[:, n, 1], Zs[:, n], start=True, stop=True)
                        last = pe.matmul(o[:, P:2 * P], Zs[:, n], TT[:, n, 1], start=True, stop=True)
                    last.then_inc(S["rw_TXT"], 1)

                z(1)
                dense(3)
                txt(1)
                dense(4)
                z(2)
                pe.wait_ge(S["at_sm"], 2 * j + 2)
                for c in range(2):
                    last = transposed(bank(4)[:, c * P:(c + 1) * P], av[:, c * P:(c + 1) * P])
                last.then_inc(S["at_vT"], 1)
                pe.wait_ge(S["at_w"], 2 * j + 2)
                for n in range(3):
                    last = transposed(bank(3)[:, n * P:(n + 1) * P], wq[:, n * P:(n + 1) * P])
                last.then_inc(S["at_wT"], 1)
                txt(2)
                dense(5)
                z(3)
                waits(pe, j + 1, "at_wt", "at_vn")
                pe.matmul(bank(3)[:, 0:P], wt[:, 0:P], avn[:, 0], start=True, stop=True)
                pe.matmul(bank(3)[:, P:2 * P], wt[:, P:2 * P], avn[:, 0], start=True, stop=False)
                pe.matmul(bank(3)[:, P:2 * P], wt[:, 2 * P:3 * P], avn[:, 1], start=False, stop=True).then_inc(S["at_o"], 1)
                dense(6)
                txt(3)
                dense(7)
                z(4)
                pe.wait_ge(S["at_on"], j + 1)
                for q in range(2):
                    last = transposed(bank(4)[:, q * P:(q + 1) * P], on[:, q])
                last.then_inc(S["at_oT"], 1)
                dense(8)
                txt(4)
                z(5)
                dense(9)
                txt(5)
                transposed(bank(5)[:, 0:P], bk[:, 1, 0:P])
                transposed(bank(5)[:, P:2 * P], bk[:, 0, 0:P]).then_inc(S["rw_kbT"], 1)
                dense(10)
                z(6)
                pe.wait_ge(S["rw_kbn"], j + 1)
                for h in range(2):
                    last = pe.matmul(bank(5)[:, 256 + 64 * h:320 + 64 * h], KTR[:, 2 * h, 0:P], Vn[:, 0, 64 * h:64 * h + 64], start=True, stop=True)
                last.then_inc(S["rw_R0"], 1)
                txt(6)
                dense(11)
                pe.wait_ge(S["rw_TT"], 7 * j + 7)
                pe.wait_ge(S["rw_nR0"], j + 1)
                for h in range(2):
                    last = pe.matmul(bank(5)[:, 384 + 64 * h:448 + 64 * h], TT[:, 2 * h, 1], nR[:, 0, 64 * h:64 * h + 64], start=True, stop=True)
                last.then_inc(S["rw_U0"], 1)
                pe.wait_ge(S["rw_Us0"], j + 1)
                pe.matmul(bank(1)[:, P:2 * P], kbn[:, 0], Vn[:, 0], start=True, stop=False)
                pe.matmul(bank(1)[:, P:2 * P], kbn[:, 1], Us[:, 0], start=False, stop=True).then_inc(S["rw_S"], 1)
                for h in range(2):
                    o, v = bank(2)[:, 256 + 64 * h:320 + 64 * h], slice(64 * h, 64 * h + 64)
                    pe.matmul(o, KTR[:, 2 * h, P:2 * P], Vn[:, 0, v], start=True, stop=False)
                    pe.matmul(o, LTR[:, 2 * h, P:2 * P], Us[:, 0, v], start=False, stop=True)
                pe.wait_ge(S["rw_S0"], j + 1)
                pe.matmul(bank(1)[:, 0:P], AR[:, 1, 0], S0, start=True, stop=False, skip_group_check=True)
                for h in range(2):
                    last = pe.matmul(bank(1)[:, 64 * h:64 * h + 64], KTR[:, 2 * h + 1, 0:P], Vn[:, 1, 64 * h:64 * h + 64],
                                     start=False, stop=True, skip_group_check=True)
                last.then_inc(S["rw_R1"], 1)
                pe.wait_ge(S["rw_nR1"], j + 1)
                for h in range(2):
                    last = pe.matmul(bank(2)[:, 64 * h:64 * h + 64], TT[:, 2 * h + 1, 1], nR[:, 1, 64 * h:64 * h + 64], start=True, stop=True)
                last.then_inc(S["rw_U1"], 1)
                pe.wait_ge(S["rw_Us1"], j + 1)
                pe.matmul(bank(2)[:, 384:512], AR[:, 1, 1], S0, start=True, stop=False, skip_group_check=True)
                for h in range(2):
                    o, v = bank(2)[:, 384 + 64 * h:448 + 64 * h], slice(64 * h, 64 * h + 64)
                    pe.matmul(o, KTR[:, 2 * h + 1, P:2 * P], Vn[:, 1, v], start=False, stop=False, skip_group_check=True)
                    last = pe.matmul(o, LTR[:, 2 * h + 1, P:2 * P], Us[:, 1, v], start=False, stop=True, skip_group_check=True)
                last.then_inc(S["rw_y"], 1)
                pe.matmul(bank(0)[:, 0:T], head_ones, rkb, start=True, stop=True).then_inc(S["rw_bonus"], 1)
                pe.wait_ge(S["rw_late"], 32 * j + 32)
                pe.matmul(bank(5)[:, 0:T], gu[0:32], sgl[0:32], start=True, stop=True).then_inc(S["rw_g"], 1)
                pe.wait_ge(S["rw_yn"], j + 1)
                for c in range(2):
                    last = transposed(bank(1)[:, 256 + c * P:256 + (c + 1) * P], flat(yc)[:, c * P:(c + 1) * P])
                last.then_inc(S["rw_yT"], 1)

            even_step(0, [Block(EVEN + 6 + u) for u in range(6)])
            with pe.Fori(0, 3) as i:
                for e in range(2):
                    even_step(1 + 2 * i + e, [Block(EVEN + 12 + 6 * e + u, i, 12) for u in range(6)])
            even_step(7, None)

            def run(base, rounds, high, low, kt=KT):
                with pe.Fori(0, rounds) as i:
                    for u in range(4):
                        for half in range(2):
                            Block(base + u, i, 4, kt=kt).products(pe, half, high, low)

            def ffn(layer):
                norm(1 + 2 * layer)
                first = FB * layer
                for m, (gate_up, down) in zip(PASSES, FFN[layer]):
                    run(gate_up, m // 2, hh, hl)
                    first += m
                    pe.wait_ge(S["hid_done"], first)
                    run(down, KT // 4, mh, ml, kt=m)

            waits(pe, NRW + 1, "rw_end", "at_end")
            run(EVEN_OUT, KT // 4, mh, ml)
            ffn(0)
            norm(2)

            def odd_step(h, blocks):
                def dense(n):
                    if blocks is not None:
                        blocks[n // 2].products(pe, n % 2, hh, hl)

                pe.wait_ge(S["hg_end"], h + 1)
                evacuated(pe, ODD + 4 * h + 3)
                for c in range(2):
                    last = transposed(bank(5)[:, c * P:(c + 1) * P], hi[:, c * P:(c + 1) * P])
                last.then_inc(S["hg_iT"], 1)
                dense(0)
                dense(1)
                dense(2)
                pe.wait_ge(S["hg_X"], 16 * h + 16)
                pe.matmul(bank(4)[:, 0:P], XX[:, 7, 0:P], XX[:, 7, P:T], start=True, stop=True)
                for l in range(7):
                    for c in range(2):
                        t = XX[:, l, c * P:(c + 1) * P]
                        pe.matmul(pm[:, l * T + c * P:l * T + (c + 1) * P], t, t, start=True, stop=True)
                for c in range(2):
                    last = pe.matmul(pm[:, 7 * T + c * P:7 * T + (c + 1) * P], hk[:, c * P:(c + 1) * P], hq[:, c * P:(c + 1) * P], start=True, stop=True)
                last.then_inc(S["hg_mm"], 1)
                dense(3)
                dense(4)
                pe.wait_ge(S["hg_AT"], 3 * h + 3)
                waits(pe, h + 1, "hg_A01", "hg_In")
                pe.matmul(bank(5)[:, 256:384], AM[:, 0, 0:P], In[:, 0], start=True, stop=True)
                pe.matmul(bank(5)[:, 384:512], A01, In[:, 0], start=True, stop=False)
                pe.matmul(bank(5)[:, 384:512], AM[:, 0, P:T], In[:, 1], start=False, stop=True).then_inc(S["hg_o"], 1)
                dense(5)
                pe.wait_ge(S["hg_on"], h + 1)
                for q in range(2):
                    last = transposed(bank(4)[:, 256 + q * P:256 + (q + 1) * P], hon[:, q])
                last.then_inc(S["hg_oT"], 1)
                dense(6)
                dense(7)

            for n in range(4):
                for half in range(2):
                    Block(ODD + n).products(pe, half, hh, hl)
            with pe.Fori(0, NHG - 1) as h:
                odd_step(h, [Block(ODD + 4 + u, h, 4) for u in range(4)])
            odd_step(NHG - 1, None)
            pe.wait_ge(S["hg_end"], NHG + 1)
            run(ODD_OUT, KT // 4, mh, ml)
            ffn(1)
            norm(4)


def kernel(x, attn_norm_g, ffn_norm_g, final_norm_g, even_w_in, even_w_out, da_lambda, da_subln_g, rw_mu, rw_w0,
           rw_w_up, rw_a0, rw_a_up, rw_g_up, rw_k_k, rw_k_a, rw_r_k, rw_ln_w, rw_ln_b, odd_w_in, odd_w_out,
           hg_lower_bound, hg_norm_g, ffn_w_gate, ffn_w_up, ffn_w_down):
    import concourse.bacc as bacc
    from concourse.bass_utils import run_bass_kernel_spmd as run

    a = np.asarray

    def blocks(w):
        w = a(w)
        return w.reshape(w.shape[0] // P, P, w.shape[1] // P, P).transpose(2, 1, 0, 3)

    def columns(v):
        return a(v).reshape(-1, P).T

    we = a(even_w_in[0])
    lowrank = blocks(np.concatenate([we[:, 6144:6304], np.zeros((D, 96), np.float32)], 1))
    cols = [blocks(we[:, n * 1024:(n + 1) * 1024]) for n in range(6)]
    order = [cols[g][j] for j in range(NRW) for g in (3, 4, 5, 0, 1, 2)]
    w_even = np.concatenate([lowrank, np.stack(order)])
    wo = blocks(odd_w_in[0]).reshape(4, NHG, P, KT, P)
    w_odd = wo[[1, 2, 3, 0]].transpose(1, 0, 2, 3, 4).reshape(4 * NHG, P, KT, P)
    w_gu = np.stack([np.stack([blocks(ffn_w_gate[i]), blocks(ffn_w_up[i])], 1).reshape(2 * FB, P, KT, P) for i in range(2)])
    w_down = np.stack([blocks(ffn_w_down[i]) for i in range(2)])
    mu = a(rw_mu[0])
    gains = np.zeros((P, NG), np.float32)
    for at, v in ((G_ATT0, attn_norm_g[0]), (G_FFN0, ffn_norm_g[0]), (G_ATT1, attn_norm_g[1]), (G_FFN1, ffn_norm_g[1]),
                  (G_FIN, final_norm_g), (G_LB0, hg_lower_bound[0]), (G_LB1, hg_lower_bound[1]), (G_SUB, da_subln_g[0]),
                  (G_HGN, hg_norm_g[0]), (G_MUW, mu[3072:3200])):
        c = columns(v)
        gains[:, at:at + c.shape[1]] = c
    gains[0:32, G_MUG] = mu[3200:3232]
    gains[:, G_LAM:G_LAM + 256] = a(da_lambda[0]).reshape(1, 256)
    par = np.stack([columns(v) for v in (mu[0:1024], mu[1024:2048], mu[2048:3072], rw_w0[0], rw_a0[0], rw_k_k[0], rw_k_a[0],
                                         a(rw_r_k[0]).reshape(-1))], 2).transpose(1, 0, 2)
    par_ln = np.stack([columns(rw_ln_w[0]), columns(rw_ln_b[0])], 2).transpose(1, 0, 2)
    wa_up = np.concatenate([a(rw_w_up[0]), a(rw_a_up[0])], 0).reshape(P, NRW, P).transpose(1, 0, 2)
    g_up = a(rw_g_up[0]).reshape(32, NRW, P).transpose(1, 0, 2)
    arrays = {
        "xT": a(x)[0].T.reshape(KT, P, T).transpose(1, 0, 2), "w_even": w_even, "w_even_out": blocks(even_w_out[0]),
        "w_odd": w_odd, "w_odd_out": blocks(odd_w_out[0]), "w_gu": w_gu, "w_down": w_down,
        "consts": shape_constants(), "gains": gains, "par": par, "par_ln": par_ln, "wa_up": wa_up, "g_up": g_up,
    }
    arrays = {k: np.ascontiguousarray(v) for k, v in arrays.items()}
    nc = bacc.Bacc("TRN2", target_bir_lowering=False, num_devices=1)
    aps = {k: nc.dram_tensor(k, v.shape, F32, kind="ExternalInput").ap() for k, v in arrays.items()}
    out = nc.dram_tensor("out", (P, KT, T), F32, kind="ExternalOutput").ap()
    build(nc, *(aps[k] for k in arrays), out)
    r = run(nc, [arrays], core_ids=[0])
    return np.ascontiguousarray(a(r.results[0]["out"]).transpose(1, 0, 2).reshape(D, T).T.reshape(1, T, D))
```

```python
from contextlib import ExitStack
import math

import numpy as np
import concourse.bass as bass
from concourse import mybir

F32 = mybir.dt.float32
F32R = mybir.dt.float32r
ACT = mybir.ActivationFunctionType
ALU = mybir.AluOpType
AX = mybir.AxisListType

P = 128
D = 2048
T = 256
KT = D // P
NRW = 8
NHG = 16
FB = 44
PASSES = (16, 16, 12)
EPS = 1e-6
GN_EPS = 64e-5
RAW, RES = 4, 2
HALF = KT // 2
LEVELS = 7
LAM_INIT = 0.8 - 0.6 * math.exp(0.0)
NEG_EXP_HALF = -math.exp(-0.5)
LOG_SHIFT = 24

C_ONES, C_HEAD, C_ROT = 0, 128, 256
C_LVL = 384
C_ID = C_LVL + LEVELS * P
C_TRI = C_ID + P
C_LOW0 = C_TRI + 2 * P
C_COS = C_LOW0 + P
C_SIN = C_COS + T
C_CAUSAL = C_SIN + T
C_END = C_CAUSAL + 3 * P
P_MU, P_W0, P_A0, P_KK, P_KA, P_RK = 0, 3, 4, 5, 6, 7
NPAR = 8
G_ATT0, G_FFN0, G_ATT1, G_FFN1, G_FIN = 0, 16, 32, 48, 64
G_LB0, G_LB1 = 80, 96
G_SUB, G_HGN, G_MUW, G_MUG = 112, 113, 114, 115
G_LAM = 116
NG = G_LAM + 256


def shape_constants():
    c = np.zeros((P, C_END), np.float32)
    i = np.arange(P)
    c[:, C_ID:C_ID + P] = np.eye(P)
    c[:, C_ONES:C_ONES + P] = 1.0
    c[:, C_HEAD:C_HEAD + P] = (i[:, None] // 64 == i[None, :] // 64)
    for comp in range(2):
        for d in range(8):
            c[64 * comp + d + 8, C_ROT + 64 * comp + d] = -1.0
            c[64 * comp + d, C_ROT + 64 * comp + d + 8] = 1.0
    s, t = i[:, None], i[None, :]
    for l in range(LEVELS):
        b = 1 << l
        m = (s // (2 * b) == t // (2 * b)) & ((s // b) % 2 == 0) & ((t // b) % 2 == 1)
        c[:, C_LVL + l * P:C_LVL + (l + 1) * P] = m
        if l == 0:
            c[:, C_LOW0:C_LOW0 + P] = m.T
    c[:, C_TRI:C_TRI + P] = s < t
    c[:, C_TRI + P:C_TRI + 2 * P] = s <= t
    inv = (1.0 / (np.float32(500000.0) ** (np.arange(0, 16, 2, dtype=np.float32) / np.float32(16)))).astype(np.float32)
    ang = (np.arange(T, dtype=np.float32)[None, :] * inv[:, None]).astype(np.float32)
    c[:, C_COS:C_COS + T] = 1.0
    for comp in range(2):
        for half in range(2):
            r = 64 * comp + 8 * half
            c[r:r + 8, C_COS:C_COS + T] = np.cos(ang)
            c[r:r + 8, C_SIN:C_SIN + T] = np.sin(ang)
    low = np.where(i[None, :] <= i[:, None], 0.0, -1e30)
    c[:, C_CAUSAL:C_CAUSAL + P] = low
    c[:, C_CAUSAL + 2 * P:C_CAUSAL + 3 * P] = low
    return c


def build(nc, xT, w_even, w_even_out, w_odd, w_odd_out, w_gu, w_down, consts, gains, par, par_ln, wa_up, g_up, out):
    with ExitStack() as ctx:
        def sb(name, shape, dt=F32):
            return ctx.enter_context(nc.sbuf_tensor(name, shape, dt))

        def sem(name):
            return ctx.enter_context(nc.semaphore(name))

        raw = sb("w_raw", [P, RAW, KT, P])
        wh = sb("w_high", [P, RES, KT, P], F32R)
        wl = sb("w_low", [P, RES, KT, P], F32R)
        hh = sb("h_high", [P, KT, T], F32R)
        hl = sb("h_low", [P, KT, T], F32R)
        mh = sb("mix_high", [P, KT, T], F32R)
        ml = sb("mix_low", [P, KT, T], F32R)
        cst = sb("constants_sb", [P, C_END])
        gn = sb("gains_sb", [P, NG])
        small = sb("small", [P, 96])
        ARENA = 17100
        arena = sb("arena", [P, ARENA])
        x = arena[:, 0:KT * T].rearrange("p (k t) -> p k t", t=T)
        used = [0]

        def take(*shape):
            n = int(np.prod(shape))
            ap = arena[:, used[0]:used[0] + n]
            used[0] += n
            assert used[0] <= ARENA, used[0]
            if len(shape) == 2:
                ap = ap.rearrange("p (a b) -> p a b", b=shape[1])
            if len(shape) == 3:
                ap = ap.rearrange("p (a b c) -> p a b c", b=shape[1], c=shape[2])
            return ap

        def flat(ap):
            return ap.rearrange("p a b -> p (a b)")

        def bc(ap, n):
            return ap.unsqueeze(1).broadcast_to([P, n, ap.shape[1]])

        r3 = take(3, T + 1)
        d3 = take(3, T)
        xm = take(3, T)
        lw = take(T)
        ag = take(T)
        b_sum = take(2, P + 1)
        e1 = take(2, P + 1)
        e2 = take(2, P)
        AR = take(2, 2, P)
        bk = take(2, T)
        rkb = take(T)
        Vn = take(2, P)
        LTR = take(4, 2 * P)
        KTR = take(4, 2 * P)
        TT = take(4, 2, P)
        Xb = take(2, 4, P)
        Zs = take(4, P)
        nR = take(2, P)
        Us = take(2, P)
        kbn = take(2, P)
        S0 = take(P)
        yc = take(4, 64)
        ysq = take(4, 64)
        yT = take(T)
        otmp = take(T)
        thw = take(T)
        sgl = take(T)
        wa = take(P)
        gu = take(P)
        pj = take(NPAR)
        pln = take(2)
        aqk = take(2, T)
        av = take(T)
        aro = take(2, T)
        qk = take(2, T)
        prob = take(2, 3 * P)
        wq = take(3 * P)
        wt = take(3 * P)
        avn = take(2, P)
        on = take(2, P)
        atmp = take(T)

        used[0] = KT * T
        hf, hi, hg, hq = take(T), take(T), take(T), take(T)
        fs = take(T)
        gsig = take(T)
        gs = take(T)
        lf = take(T)
        hb = take(T)
        hk = take(T)
        DD = take(8, T)
        XX = take(8, T)
        AM = take(6, T)
        A01 = take(P)
        In = take(2, P)
        hon = take(2, P)
        htmp = take(T)
        hpar = take(2)
        used[0] = KT * T
        sil = take(2, T)
        hid32 = take(2, T)
        nsq = take(4, T)
        nss = take(T)
        nrs = take(T)
        n32 = take(2, T)
        lamv = take(2, 64)

        ident = cst[:, C_ID:C_ID + P]
        ones = cst[:, C_ONES:C_ONES + P]
        head_ones = cst[:, C_HEAD:C_HEAD + P]
        rot = cst[:, C_ROT:C_ROT + P]

        def level_mask(l):
            return cst[:, C_LVL + l * P:C_LVL + (l + 1) * P]

        c_eps, c_gn, c_ln08, c_shift = (small[:, i:i + 1] for i in range(4))
        nlam = small[:, 7:8]
        lamt = small[:, 8:12]
        omka = small[:, 12:13]
        nbm = small[:, 13:15]
        pbm = small[:, 15:17]
        ebm = small[:, 17:18]
        scl = small[:, 18:19]
        ymean = small[:, 20:24]
        yvar = small[:, 24:28]
        yrs = small[:, 32:36]
        amx = small[:, 36:40]
        anb = small[:, 40:44]
        asum = small[:, 44:48]
        ass = small[:, 52:54]
        aln = small[:, 54:56]
        ars = small[:, 56:58]
        hlb = small[:, 60:76]
        homl = small[:, 76:92]

        acc = [ctx.enter_context(nc.psum_tensor(f"acc{i}", [P, 512], F32)) for i in range(2)]
        pm = ctx.enter_context(nc.psum_tensor("mixer_banks", [P, 6 * 512], F32))

        def bank(b, n=1):
            return pm[:, b * 512:(b + n) * 512]

        landed = [sem(f"w_landed{i}") for i in range(RAW)]
        high_done = sem("w_high_done")
        low_done = sem("w_low_done")
        half_done = sem("half_products_done")
        evac_done = sem("product_evacuated")
        S = {}
        for group in (
            "consts_in x_in x_back credits sq sq_sum sq_total norm_ln norm_rstd h32 h_high h_low out_done",
            "lam_vec lam_sum lam_exp lb_diff lb one_minus_lb",
            "low_zero low_diff low_mixed low_acts",
            "hid_high hid_done base_mask",
            "rw_par rw_late rw_d rw_xr rw_xk rw_xv rw_za rw_sig rw_a rw_lw rw_b rw_mid rw_e1 rw_e2 rw_ebm rw_scl rw_omka rw_sq rw_kk",
            "rw_ss rw_ssmax rw_ssln rw_rn rw_kkn rw_t1 rw_k2 rw_at rw_kka rw_bt rw_kt rw_rt rw_rk rw_bonus rw_bv rw_vt rw_vn",
            "rw_m1 rw_m2 rw_m3 rw_LTR rw_KTR rw_T0 rw_TT rw_X rw_Z rw_Zs rw_TXT rw_kbT rw_kbn rw_R0 rw_nR0 rw_U0 rw_Us0",
            "rw_S rw_S0 rw_R1 rw_nR1 rw_U1 rw_Us1 rw_y rw_ymean rw_yc rw_ysq rw_yvar rw_yln rw_yrs rw_yn rw_yT rw_yTs",
            "rw_sum rw_g rw_out rw_hi rw_end",
            "at_rot at_sin at_cos at_qk at_s at_sm at_mx at_nb at_p at_rc at_w0 at_w at_wT at_wt at_vT at_vn at_o at_ss at_ln",
            "at_rs at_on at_oT at_out at_hi at_end",
            "hg_par hg_sig hg_silu hg_lf hg_k hg_b hg_D hg_E hg_X hg_mm hg_AM hg_AT hg_A01 hg_iT hg_In hg_o hg_ss",
            "hg_ln hg_rs hg_on hg_oT hg_out hg_hi hg_end",
        ):
            for name in group.split():
                S[name] = sem(name)

        def waits(eng, count, *names):
            for name in names:
                eng.wait_ge(S[name], count)

        class Block:

            def __init__(self, base, i=None, step=0, kt=KT):
                self.kt = kt
                self.n = base if i is None else base + step * i
                self.loads = base // RAW + 1 if i is None else base // RAW + 1 + step // RAW * i
                self.raw, self.res, self.acc = base % RAW, base % RES, base % 2

            def load(self, sp, src):
                sp.wait_ge(low_done, 2 * self.n + 2)
                sp.dma_start(raw[:, self.raw, 0:self.kt], src).then_inc(landed[self.raw], 16)

            def high(self, act, half):
                ks = slice(half * HALF, half * HALF + HALF)
                act.wait_ge(landed[self.raw], self.loads * 16)
                act.wait_ge(half_done, 2 * self.n + half + 1)
                act.activation(wh[:, self.res, ks], raw[:, self.raw, ks], ACT.Copy).then_inc(high_done, 1)

            def low(self, dve, half):
                ks = slice(half * HALF, half * HALF + HALF)
                dve.wait_ge(high_done, 2 * self.n + half + 1)
                dve.tensor_tensor(wl[:, self.res, ks], raw[:, self.raw, ks],
                                  wh[:, self.res, ks].bitcast(F32), ALU.subtract).then_inc(low_done, 1)

            def tile(self, pe, k, high, low, incs=(1, 1)):
                if k % HALF == 0:
                    pe.wait_ge(low_done, 2 * self.n + k // HALF + 1 + 2 * RAW)
                if k == 0:
                    pe.wait_ge(evac_done, self.n + 1)
                o = acc[self.acc][:, 0:T]
                pe.matmul(o, wh[:, self.res, k], high[:, k], start=k == 0, stop=False)
                pe.matmul(o, wh[:, self.res, k], low[:, k], start=False, stop=False)
                last = pe.matmul(o, wl[:, self.res, k], high[:, k], start=False, stop=k == self.kt - 1)
                if k % HALF == HALF - 1 or k == self.kt - 1:
                    if incs[k // HALF]:
                        last.then_inc(half_done, incs[k // HALF])

            def products(self, pe, half, high, low):
                for k in range(half * HALF, min(self.kt, half * HALF + HALF)):
                    self.tile(pe, k, high, low)

            def result(self, eng):
                eng.wait_ge(half_done, 2 * self.n + 2 + 2 * RES)
                return acc[self.acc][:, 0:T]

            def wait_evacuated(self, eng):
                eng.wait_ge(evac_done, self.n + 1 + 2)

        LOWRANK = 0
        EVEN = 2
        EVEN_OUT = EVEN + 6 * NRW
        FFN = []
        n = EVEN_OUT + KT
        for layer in range(2):
            at = []
            for m in PASSES:
                at.append((n, n + 2 * m))
                n += 2 * m + KT
            FFN.append(at)
            if layer == 0:
                ODD = n
                ODD_OUT = ODD + 4 * NHG
                n = ODD_OUT + KT

        TOTAL = n

        def evacuated(eng, n):
            eng.wait_ge(evac_done, n + 1 + 2)

        block = ctx.enter_context(nc.Block())

        @block.sync
        def _(sp):
            sp.dma_start(cst[:], consts).then_inc(S["consts_in"], 16)
            sp.dma_start(gn[:], gains).then_inc(S["consts_in"], 16)
            for q in range(4):
                sp.dma_start(x[:, 4 * q:4 * q + 4], xT[:, 4 * q:4 * q + 4]).then_inc(S["x_in"], 16)
            for n in range(LOWRANK, EVEN + 6):
                Block(n).load(sp, w_even[n])
            with sp.Fori(0, 3) as i:
                for u in range(12):
                    Block(EVEN + 6 + u, i, 12).load(sp, w_even[EVEN + 6 + u + 12 * i])
            for n in range(EVEN + 42, EVEN + 48):
                Block(n).load(sp, w_even[n])

            def square(base, w):
                with sp.Fori(0, KT // 4) as i:
                    for u in range(4):
                        Block(base + u, i, 4).load(sp, w[u + 4 * i])

            def ffn(layer):
                first = 0
                for m, (gate_up, down) in zip(PASSES, FFN[layer]):
                    with sp.Fori(0, m // 2) as i:
                        for u in range(4):
                            Block(gate_up + u, i, 4).load(sp, w_gu[layer][2 * first + u + 4 * i])
                    with sp.Fori(0, KT // 4) as i:
                        for u in range(4):
                            Block(down + u, i, 4, kt=m).load(sp, w_down[layer][u + 4 * i][:, first:first + m])
                    first += m

            square(EVEN_OUT, w_even_out)
            ffn(0)
            with sp.Fori(0, NHG) as i:
                for u in range(4):
                    Block(ODD + u, i, 4).load(sp, w_odd[u + 4 * i])
            square(ODD_OUT, w_odd_out)
            ffn(1)
            for q in range(4):
                sp.wait_ge(S["h32"], 4 * KT + 4 * q + 4)
                sp.dma_start(out[:, 4 * q:4 * q + 4], x[:, 4 * q:4 * q + 4]).then_inc(S["out_done"], 16)
            sp.wait_ge(S["out_done"], 64)

        @block.gpsimd
        def _(pool):
            def even_step(j):
                evacuated(pool, EVEN + 6 * j + 4)
                pool.wait_ge(S["at_end"], j + 1)
                for c in range(2):
                    pool.tensor_tensor(qk[:, c], aqk[:, c], cst[:, C_COS:C_COS + T], ALU.mult).then_inc(S["at_cos"], 1)
                pool.wait_ge(S["rw_LTR"], 2 * j + 2)
                for l in range(1, LEVELS):
                    pool.wait_ge(S["rw_Z"], 6 * j + max(l - 2, 0))
                    pool.tensor_tensor(Xb[:, l % 2], LTR[:, :, 0:P], bc(level_mask(l), 4), ALU.mult).then_inc(S["rw_X"], 1)

            pool.wait_ge(S["consts_in"], 32)
            even_step(0)
            with pool.Fori(0, 3) as i:
                for e in range(2):
                    even_step(1 + 2 * i + e)
            even_step(7)
            waits(pool, NRW + 1, "rw_end", "at_end")
            pool.dma_start(x, xT).then_inc(S["x_back"], 16)

        @block.scalar
        def _(act):
            def norm(m):
                act.wait_ge(S["sq_total"], m + 1)
                act.activation(nrs, bank(0)[:, 0:T], ACT.Ln, bias=c_eps, scale=1.0 / D).then_inc(S["norm_ln"], 1)
                act.wait_ge(S["norm_ln"], m + 1)
                act.activation(nrs, nrs, ACT.Exp, scale=-0.5).then_inc(S["norm_rstd"], 1)
                for k in range(KT if m < 4 else 0):
                    act.wait_ge(S["h32"], m * KT + k + 1)
                    act.activation(hh[:, k], n32[:, k % 2], ACT.Copy).then_inc(S["h_high"], 1)

            waits(act, 1, "credits")
            act.wait_ge(S["lam_sum"], 1)
            act.activation(lamt[:, 2:4], lamt[:, 0:2], ACT.Exp).then_inc(S["lam_exp"], 1)
            act.wait_ge(S["lb_diff"], 1)
            act.activation(hlb, homl, ACT.Sigmoid).then_inc(S["lb"], 1)
            act.preload_act_table_set("natural_log_exp_and_others")
            for k in range(KT):
                act.wait_ge(S["x_in"], 64)
                if k >= 4:
                    act.wait_ge(S["sq_sum"], k - 2)
                act.activation(nsq[:, k % 4], x[:, k], ACT.Square).then_inc(S["sq"], 1)
            norm(0)
            act.dma_start(wa, wa_up[0]).then_inc(S["rw_par"], 16)
            act.dma_start(pj, par[0]).then_inc(S["rw_par"], 16)
            act.dma_start(gu[0:32], g_up[0]).then_inc(S["rw_late"], 16)
            act.dma_start(pln, par_ln[0]).then_inc(S["rw_late"], 16)
            for n in range(2):
                for half in range(2):
                    Block(LOWRANK + n).high(act, half)
            for n in range(2):
                Block(LOWRANK + n + 2).high(act, 0)
                product = Block(LOWRANK + n).result(act)
                act.wait_ge(S["low_zero"], 2)
                act.activation(r3[:, n, 1:], product, ACT.Copy).then_inc(evac_done, 1)
                Block(LOWRANK + n + 2).high(act, 1)
            act.wait_ge(S["low_mixed"], 2)
            act.activation(thw[0:64], xm[0:64, 0], ACT.Tanh).then_inc(S["low_acts"], 1)
            act.activation(thw[64:128], xm[64:128, 0], ACT.Copy).then_inc(S["low_acts"], 1)
            act.activation(sgl[0:32], xm[0:32, 1], ACT.Sigmoid).then_inc(S["low_acts"], 1)
            act.wait_ge(S["low_acts"], 3)

            def feed(this, ahead, dst, wait=None):
                ahead.high(act, 0)
                product = this.result(act)
                if wait:
                    wait()
                act.activation(dst, product, ACT.Copy).then_inc(evac_done, 1)
                ahead.high(act, 1)

            even_dst = [r3[:, 0, 1:], r3[:, 1, 1:], r3[:, 2, 1:], aqk[:, 0], aqk[:, 1], av]

            def even_feed(u, blocks, j):
                if blocks is None:
                    return

                def wait():
                    if u < 3:
                        act.wait_ge(S["rw_xv"], j + 1)
                    elif u < 5:
                        act.wait_ge(S["at_rot"], j + 1)
                        act.wait_ge(S["at_cos"], 2 * j + 2)
                    else:
                        act.wait_ge(S["at_vT"], j + 1)
                feed(blocks[u], blocks[u + 2], even_dst[u], wait)

            def even_step(j, blocks):
                act.wait_ge(S["rw_za"], j + 1)
                act.activation(lw, bank(5)[:, 0:T], ACT.Sigmoid, bias=pj[:, P_W0:P_W0 + 1]).then_inc(S["rw_sig"], 1)
                act.activation(ag, bank(0)[:, 0:T], ACT.Sigmoid, bias=pj[:, P_A0:P_A0 + 1]).then_inc(S["rw_a"], 1)
                act.wait_ge(S["rw_xv"], j + 1)
                act.activation(d3[:, 2], xm[:, 1], ACT.Square, scale=pj[:, P_KK:P_KK + 1]).then_inc(S["rw_sq"], 1)
                act.wait_ge(S["rw_b"], 2 * j + 2)
                act.wait_ge(S["rw_mid"], 2 * j + 2)
                for c in range(2):
                    act.activation(e1[:, c], b_sum[:, c], ACT.Exp, bias=nbm[:, c:c + 1]).then_inc(S["rw_e1"], 1)
                    act.activation(e2[:, c], b_sum[:, c, 1:], ACT.Exp, bias=pbm[:, c:c + 1], scale=-1.0).then_inc(S["rw_e2"], 1)
                act.activation(ebm, pbm[:, 1:2], ACT.Exp).then_inc(S["rw_ebm"], 1)
                act.wait_ge(S["rw_ssmax"], j + 1)
                act.activation(d3[:, 2], d3[:, 2], ACT.Ln, scale=2.0 ** LOG_SHIFT).then_inc(S["rw_ssln"], 1)
                act.wait_ge(S["rw_ssln"], j + 1)
                act.activation(d3[:, 2], d3[:, 2], ACT.Exp, scale=-0.5, bias=c_shift).then_inc(S["rw_rn"], 1)
                act.wait_ge(S["rw_vt"], j + 1)
                act.activation(flat(Vn), bank(4)[:, 256:512], ACT.Copy).then_inc(S["rw_vn"], 1)
                if blocks is not None:
                    waits(act, j + 1, "rw_rk", "rw_t1", "rw_kk", "rw_sq", "rw_a")
                    act.dma_start(wa, wa_up[j + 1]).then_inc(S["rw_par"], 16)
                    act.dma_start(pj, par[j + 1]).then_inc(S["rw_par"], 16)

                def z_copy(l):
                    act.wait_ge(S["rw_Z"], 6 * j + l)
                    act.activation(flat(Zs), bank(2), ACT.Copy).then_inc(S["rw_Zs"], 1)

                even_feed(0, blocks, j)
                z_copy(1)
                act.wait_ge(S["at_nb"], j + 1)
                for q, cols in enumerate((slice(0, P), slice(P, 3 * P))):
                    for c in range(2):
                        n = 2 * q + c
                        act.activation(prob[:, c, cols], prob[:, c, cols], ACT.Exp, bias=anb[:, n:n + 1], scale=0.125,
                                       accum_out=asum[:, n:n + 1]).then_inc(S["at_p"], 1)
                even_feed(1, blocks, j)
                z_copy(2)
                act.wait_ge(S["at_wT"], j + 1)
                act.activation(wt, bank(3)[:, 0:384], ACT.Copy).then_inc(S["at_wt"], 1)
                act.wait_ge(S["at_vT"], j + 1)
                act.activation(flat(avn), bank(4)[:, 0:256], ACT.Copy).then_inc(S["at_vn"], 1)
                even_feed(2, blocks, j)
                z_copy(3)
                act.wait_ge(S["at_o"], j + 1)
                for q in range(2):
                    act.activation(on[:, q], bank(3)[:, q * P:(q + 1) * P], ACT.Square, accum_out=ass[:, q:q + 1]).then_inc(S["at_ss"], 1)
                act.wait_ge(S["at_ss"], 2 * j + 2)
                act.activation(aln, ass, ACT.Ln, scale=1.0 / P, bias=c_eps).then_inc(S["at_ln"], 1)
                act.wait_ge(S["at_ln"], j + 1)
                act.activation(ars, aln, ACT.Exp, scale=-0.5, bias=c_ln08).then_inc(S["at_rs"], 1)
                even_feed(3, blocks, j)
                z_copy(4)
                even_feed(4, blocks, j)
                z_copy(5)
                act.wait_ge(S["rw_kbT"], j + 1)
                act.activation(flat(kbn), bank(5)[:, 0:256], ACT.Copy).then_inc(S["rw_kbn"], 1)
                z_copy(6)
                act.wait_ge(S["rw_R0"], j + 1)
                act.activation(nR[:, 0], bank(5)[:, 256:384], ACT.Copy, scale=-1.0).then_inc(S["rw_nR0"], 1)
                even_feed(5, blocks, j)
                act.wait_ge(S["rw_U0"], j + 1)
                act.activation(Us[:, 0], bank(5)[:, 384:512], ACT.Copy).then_inc(S["rw_Us0"], 1)
                act.wait_ge(S["rw_R1"], j + 1)
                act.activation(nR[:, 1], bank(1)[:, 0:P], ACT.Copy, scale=-1.0).then_inc(S["rw_nR1"], 1)
                act.wait_ge(S["rw_U1"], j + 1)
                act.activation(Us[:, 1], bank(2)[:, 0:P], ACT.Copy).then_inc(S["rw_Us1"], 1)
                act.wait_ge(S["rw_yc"], j + 1)
                act.activation(ysq, yc, ACT.Square).then_inc(S["rw_ysq"], 1)
                act.wait_ge(S["rw_yvar"], j + 1)
                act.activation(yrs, yvar, ACT.Ln, scale=1.0 / 64, bias=c_gn).then_inc(S["rw_yln"], 1)
                act.wait_ge(S["rw_yln"], j + 1)
                act.activation(yrs, yrs, ACT.Exp, scale=-0.5).then_inc(S["rw_yrs"], 1)
                act.wait_ge(S["rw_yT"], j + 1)
                act.wait_ge(S["rw_late"], 32 * j + 32)
                act.activation(yT, bank(1)[:, 256:512], ACT.Identity, scale=pln[:, 0:1], bias=pln[:, 1:2]).then_inc(S["rw_yTs"], 1)
                if blocks is not None:
                    waits(act, j + 1, "rw_yTs", "rw_g")
                    act.dma_start(gu[0:32], g_up[j + 1]).then_inc(S["rw_late"], 16)
                    act.dma_start(pln, par_ln[j + 1]).then_inc(S["rw_late"], 16)

            for u in range(6):
                feed(Block(EVEN + u), Block(EVEN + u + 2), even_dst[u])
            even_step(0, [Block(EVEN + 6 + u) for u in range(8)])
            with act.Fori(0, 3) as i:
                for e in range(2):
                    even_step(1 + 2 * i + e, [Block(EVEN + 12 + 6 * e + u, i, 12) for u in range(8)])
            even_step(7, None)

            def square(base, before_norm=False):
                if before_norm:
                    act.preload_act_table_set("natural_log_exp_and_others")
                at_end = base + KT == TOTAL
                with act.Fori(0, KT // 4 - at_end) as i:
                    for u in range(4):
                        for half in range(2):
                            Block(base + 2 + u, i, 4).high(act, half)
                for n in range(TOTAL - 2, TOTAL if at_end else 0):
                    for half in range(2):
                        Block(n).high(act, half)

            def ffn(layer):
                norm(1 + 2 * layer)
                first = 0
                for m, (gate_up, down) in zip(PASSES, FFN[layer]):
                    with act.Fori(0, m // 2) as i:
                        for b in range(2):
                            gate = Block(gate_up + 2 * b, i, 4)
                            Block(gate_up + 2 * b + 2, i, 4).high(act, 0)
                            product = gate.result(act)
                            act.wait_ge(evac_done, gate.n + 2)
                            act.activation(sil[:, b], product, ACT.Silu).then_inc(evac_done, 1)
                            Block(gate_up + 2 * b + 2, i, 4).high(act, 1)
                            for half in range(2):
                                Block(gate_up + 2 * b + 3, i, 4).high(act, half)
                    first += m
                    square(down, before_norm=first == FB)

            square(EVEN_OUT, before_norm=True)
            ffn(0)
            norm(2)
            head_dst = [hf, hi, hg, hq]

            def gates():
                act.activation(fs, hf, ACT.Sigmoid).then_inc(S["hg_sig"], 1)
                act.activation(gsig, hg, ACT.Sigmoid).then_inc(S["hg_sig"], 1)

            def odd_step(h, last=False):
                blocks = [Block(ODD + 4 + u, h, 4) for u in range(5)]
                act.preload_act_table_set("natural_log_exp_and_others")
                act.wait_ge(S["hg_par"], 2 * h + 2)
                act.wait_ge(S["hg_sig"], 2 * h + 1)
                act.activation(lf, fs, ACT.Ln, scale=hpar[:, 1:2], bias=hpar[:, 0:1]).then_inc(S["hg_lf"], 1)
                blocks[1].high(act, 0)
                act.activation(hq, Block(ODD + 3, h, 4).result(act), ACT.Copy).then_inc(evac_done, 1)
                act.wait_ge(S["hg_iT"], h + 1)
                act.activation(flat(In), bank(5)[:, 0:256], ACT.Copy).then_inc(S["hg_In"], 1)
                blocks[1].high(act, 1)
                act.wait_ge(S["hg_D"], 13 * h + 7)
                act.activation(DD[:, 7], DD[:, 0], ACT.Exp, scale=-1.0).then_inc(S["hg_E"], 1)
                act.wait_ge(S["hg_E"], 3 * h + 1)
                act.activation(DD[:, 0:4], DD[:, 0:4], ACT.Exp).then_inc(S["hg_E"], 1)
                if not last:
                    blocks[2].high(act, 0)
                act.wait_ge(S["hg_D"], 13 * h + 13)
                act.activation(DD[:, 4:7], DD[:, 4:7], ACT.Exp).then_inc(S["hg_E"], 1)
                if not last:
                    blocks[2].high(act, 1)
                    act.activation(hf, blocks[0].result(act), ACT.Copy).then_inc(evac_done, 1)
                    blocks[3].high(act, 0)
                    blocks[3].high(act, 1)
                    act.activation(hi, blocks[1].result(act), ACT.Copy).then_inc(evac_done, 1)
                    blocks[4].high(act, 0)
                act.wait_ge(S["hg_o"], h + 1)
                for q in range(2):
                    act.activation(hon[:, q], bank(5)[:, 256 + q * P:256 + (q + 1) * P], ACT.Square,
                                   accum_out=ass[:, q:q + 1]).then_inc(S["hg_ss"], 1)
                act.wait_ge(S["hg_ss"], 2 * h + 2)
                act.activation(aln, ass, ACT.Ln, scale=1.0 / P, bias=c_eps).then_inc(S["hg_ln"], 1)
                act.wait_ge(S["hg_ln"], h + 1)
                act.activation(ars, aln, ACT.Exp, scale=-0.5).then_inc(S["hg_rs"], 1)
                if not last:
                    product = blocks[2].result(act)
                    act.wait_ge(S["hg_silu"], h + 1)
                    act.wait_ge(S["hg_k"], h + 1)
                    act.activation(hg, product, ACT.Copy).then_inc(evac_done, 1)
                    blocks[4].high(act, 1)
                    evacuated(act, ODD + 4 * h + 6)
                    gates()

            for u in range(3):
                feed(Block(ODD + u), Block(ODD + u + 2), head_dst[u])
            evacuated(act, ODD + 2)
            gates()
            with act.Fori(0, NHG - 1) as h:
                odd_step(h)
            odd_step(NHG - 1, last=True)
            square(ODD_OUT, before_norm=True)
            ffn(1)
            norm(4)

        @block.vector
        def _(dve):
            def add_square(m, k, u):
                dve.wait_ge(S["sq"], m * KT + k + 1)
                dve.wait_ge(S["sq_sum"], m * (KT + 1) + k + 1)
                dve.tensor_tensor(nss, nss, nsq[:, u], ALU.add).then_inc(S["sq_sum"], 1)

            def norm(m, gain):
                dve.wait_ge(S["norm_rstd"], m + 1)
                for k in range(KT):
                    g = gn[:, gain + k:gain + k + 1]
                    if m == 4:
                        dve.scalar_tensor_tensor(x[:, k], x[:, k], g, nrs, ALU.mult, ALU.mult).then_inc(S["h32"], 1)
                        continue
                    if k >= 2:
                        dve.wait_ge(S["h_low"], m * KT + k - 1)
                    dve.scalar_tensor_tensor(n32[:, k % 2], x[:, k], g, nrs, ALU.mult, ALU.mult).then_inc(S["h32"], 1)
                    for kk in ([k - 1] if k else []) + ([k] if k == KT - 1 else []):
                        dve.wait_ge(S["h_high"], m * KT + kk + 1)
                        dve.tensor_tensor(hl[:, kk], n32[:, kk % 2], hh[:, kk].bitcast(F32), ALU.subtract).then_inc(S["h_low"], 1)

            dve.sem_inc(low_done, 2 * RAW)
            for name in ("rw_end", "at_end", "hg_end"):
                dve.sem_inc(S[name], 1)
            dve.memset(c_eps, EPS)
            dve.memset(c_gn, GN_EPS)
            dve.memset(c_ln08, math.log(1.0 - LAM_INIT))
            dve.memset(c_shift, LOG_SHIFT / 2 * math.log(2.0)).then_inc(S["credits"], 1)
            dve.wait_ge(S["consts_in"], 32)
            dve.tensor_tensor(homl, gn[:, G_LB1:G_LB1 + 16], gn[:, G_LB0:G_LB0 + 16], ALU.subtract).then_inc(S["lb_diff"], 1)
            l4 = gn[:, G_LAM:G_LAM + 256].rearrange("p (a b c) -> p a b c", a=2, b=2)
            dve.tensor_tensor(lamv, l4[:, :, 0], l4[:, :, 1], ALU.mult).then_inc(S["lam_vec"], 1)
            dve.wait_ge(S["lam_vec"], 1)
            dve.reduce_sum(lamt[:, 0:2], lamv, AX.X).then_inc(S["lam_sum"], 1)
            dve.wait_ge(S["lam_exp"], 1)
            dve.tensor_tensor(lamt[:, 0:1], lamt[:, 3:4], lamt[:, 2:3], ALU.subtract).then_inc(S["lam_vec"], 1)
            dve.wait_ge(S["lam_vec"], 2)
            dve.tensor_scalar(nlam, lamt[:, 0:1], -LAM_INIT, None, ALU.add).then_inc(S["lam_vec"], 1)
            dve.wait_ge(S["lb"], 1)
            dve.tensor_scalar(homl, hlb, -1.0, 1.0, ALU.mult, ALU.add).then_inc(S["one_minus_lb"], 1)
            dve.wait_ge(S["lam_vec"], 3)
            dve.wait_ge(S["one_minus_lb"], 1)
            dve.memset(nss, 0.0).then_inc(S["sq_sum"], 1)
            for k in range(KT):
                add_square(0, k, k % 4)
            norm(0, G_ATT0)
            dve.wait_ge(S["h_low"], KT)
            dve.memset(r3[:, :, 0:1], 0.0).then_inc(S["low_zero"], 1)
            dve.memset(b_sum[:, :, 0:1], 0.0).then_inc(S["low_zero"], 1)
            for n in range(2):
                for half in range(2):
                    Block(LOWRANK + n).low(dve, half)
            for n in range(2):
                Block(LOWRANK + n + 2).low(dve, 0)
                Block(LOWRANK + n).wait_evacuated(dve)
                dve.tensor_tensor(d3[:, n], r3[:, n, 0:T], r3[:, n, 1:], ALU.subtract).then_inc(S["low_diff"], 1)
                dve.wait_ge(S["low_diff"], n + 1)
                dve.scalar_tensor_tensor(xm[:, n], d3[:, n], gn[:, G_MUW + n:G_MUW + n + 1], r3[:, n, 1:],
                                         ALU.mult, ALU.add).then_inc(S["low_mixed"], 1)
                Block(LOWRANK + n + 2).low(dve, 1)

            def even_step(j, blocks):
                def low(u):
                    if blocks is not None:
                        for half in range(2):
                            blocks[u + 2].low(dve, half)

                evacuated(dve, EVEN + 6 * j + 2)
                dve.wait_ge(S["rw_end"], j + 1)
                dve.wait_ge(S["rw_par"], 32 * j + 32)
                dve.tensor_tensor(d3, r3[:, :, 0:T], r3[:, :, 1:], ALU.subtract).then_inc(S["rw_d"], 1)
                dve.tensor_scalar(omka, pj[:, P_KA:P_KA + 1], -1.0, 1.0, ALU.mult, ALU.add).then_inc(S["rw_omka"], 1)
                dve.wait_ge(S["rw_d"], j + 1)
                for c, name in ((1, "rw_xk"), (0, "rw_xr"), (2, "rw_xv")):
                    dve.scalar_tensor_tensor(xm[:, c], d3[:, c], pj[:, P_MU + c:P_MU + c + 1], r3[:, c, 1:],
                                             ALU.mult, ALU.add).then_inc(S[name], 1)
                dve.wait_ge(S["rw_sig"], j + 1)
                dve.tensor_scalar(lw, lw, NEG_EXP_HALF, None, ALU.mult).then_inc(S["rw_lw"], 1)
                waits(dve, j + 1, "rw_xk", "rw_xr", "rw_xv")
                dve.tensor_scalar(d3[:, 1], xm[:, 1], pj[:, P_KK:P_KK + 1], None, ALU.mult).then_inc(S["rw_kk"], 1)
                dve.wait_ge(S["rw_lw"], j + 1)
                for c in range(2):
                    dve.tensor_tensor_scan(b_sum[:, c, 1:], ones, lw[:, c * P:(c + 1) * P], 0.0, ALU.mult, ALU.add).then_inc(S["rw_b"], 1)
                dve.wait_ge(S["rw_b"], 2 * j + 2)
                mid = b_sum[:, :, P // 2]
                dve.tensor_scalar(nbm, mid, -1.0, None, ALU.mult).then_inc(S["rw_mid"], 1)
                dve.tensor_scalar(pbm, mid, 1.0, None, ALU.mult).then_inc(S["rw_mid"], 1)
                waits(dve, j + 1, "rw_ss", "rw_sq")
                dve.tensor_scalar(d3[:, 2], bank(2)[:, 0:T], 1e-24, None, ALU.max).then_inc(S["rw_ssmax"], 1)
                waits(dve, j + 1, "rw_a", "rw_omka")
                dve.tensor_scalar(d3[:, 0], ag, pj[:, P_KA:P_KA + 1], omka, ALU.mult, ALU.add).then_inc(S["rw_t1"], 1)
                dve.wait_ge(S["rw_t1"], j + 1)
                dve.tensor_tensor(d3[:, 0], d3[:, 0], xm[:, 1], ALU.mult).then_inc(S["rw_k2"], 1)
                dve.wait_ge(S["rw_k2"], j + 1)
                dve.scalar_tensor_tensor(rkb, xm[:, 0], pj[:, P_RK:P_RK + 1], d3[:, 0], ALU.mult, ALU.mult).then_inc(S["rw_rk"], 1)
                dve.wait_ge(S["rw_e2"], 2 * j + 2)
                dve.tensor_tensor(bk[:, 1], d3[:, 0], flat(e2), ALU.mult).then_inc(S["rw_kt"], 1)
                dve.wait_ge(S["rw_e1"], 2 * j + 2)
                dve.tensor_tensor(AR[:, :, 1], xm[:, 0].rearrange("p (c t) -> p c t", c=2), e1[:, :, 1:], ALU.mult).then_inc(S["rw_rt"], 1)
                waits(dve, j + 1, "rw_rn", "rw_kk")
                dve.tensor_tensor(d3[:, 1], d3[:, 1], d3[:, 2], ALU.mult).then_inc(S["rw_kkn"], 1)
                dve.wait_ge(S["rw_kkn"], j + 1)
                dve.tensor_tensor(AR[:, :, 0], d3[:, 1].rearrange("p (c t) -> p c t", c=2), e1[:, :, 0:P], ALU.mult).then_inc(S["rw_at"], 1)
                dve.tensor_tensor(d3[:, 2], d3[:, 1], ag, ALU.mult).then_inc(S["rw_kka"], 1)
                dve.wait_ge(S["rw_kka"], j + 1)
                dve.tensor_tensor(bk[:, 0], d3[:, 2], flat(e2), ALU.mult).then_inc(S["rw_bt"], 1)
                dve.wait_ge(S["rw_ebm"], j + 1)
                dve.tensor_tensor(scl, ebm, e1[:, 0, P:P + 1], ALU.mult).then_inc(S["rw_scl"], 1)
                dve.wait_ge(S["at_rot"], j + 1)
                dve.tensor_tensor(aro, bank(3).rearrange("p (a b) -> p a b", a=2), bc(cst[:, C_SIN:C_SIN + T], 2), ALU.mult).then_inc(S["at_sin"], 1)
                dve.wait_ge(S["at_sin"], j + 1)
                dve.wait_ge(S["at_cos"], 2 * j + 2)
                dve.tensor_tensor(qk, qk, aro, ALU.add).then_inc(S["at_qk"], 1)
                low(0)
                tri = bc(cst[:, C_TRI:C_TRI + 2 * P], 2)
                dve.wait_ge(S["rw_m1"], j + 1)
                for n in range(2):
                    dve.tensor_tensor(LTR[:, 2 * n:2 * n + 2], bank(n).rearrange("p (a b) -> p a b", a=2), tri, ALU.mult).then_inc(S["rw_LTR"], 1)
                dve.wait_ge(S["rw_m3"], j + 1)
                for h in range(2):
                    dve.tensor_tensor(TT[:, 2 * h:2 * h + 2, 0], bank(5 - h)[:, 0:T].rearrange("p (a b) -> p a b", a=2),
                                      bc(cst[:, C_LOW0:C_LOW0 + P], 2), ALU.mult).then_inc(S["rw_T0"], 1)
                dve.wait_ge(S["rw_LTR"], 2 * j + 2)
                dve.tensor_tensor(TT[:, :, 1], LTR[:, :, 0:P], bc(level_mask(0), 4), ALU.mult).then_inc(S["rw_T0"], 1)
                dve.wait_ge(S["rw_T0"], 3 * j + 3)
                t8 = TT.rearrange("p a b c -> p (a b) c")
                dve.tensor_tensor(t8, bc(ident, 8), t8, ALU.subtract).then_inc(S["rw_TT"], 1)
                dve.wait_ge(S["rw_m2"], j + 1)
                for n in range(2):
                    dve.tensor_tensor(KTR[:, 2 * n:2 * n + 2], bank(2 + n).rearrange("p (a b) -> p a b", a=2), tri, ALU.mult).then_inc(S["rw_KTR"], 1)

                def level(l):
                    dve.wait_ge(S["rw_TXT"], 6 * j + l)
                    if l < LEVELS - 1:
                        t = TT.rearrange("p a b c -> p (a b c)")
                        dve.tensor_tensor(t, t, bank(0, 2), ALU.subtract).then_inc(S["rw_TT"], 1)
                    else:
                        t = TT[:, :, 1]
                        dve.tensor_tensor(t, t, bank(0, 2).rearrange("p (a b c) -> p a b c", a=4, b=2)[:, :, 1], ALU.subtract).then_inc(S["rw_TT"], 1)

                dve.wait_ge(S["at_s"], j + 1)
                for c in range(2):
                    dve.tensor_tensor(prob[:, c], bank(4 + c)[:, 0:384], cst[:, C_CAUSAL:C_END], ALU.add).then_inc(S["at_sm"], 1)
                dve.wait_ge(S["at_sm"], 2 * j + 2)
                dve.reduce_max(amx[:, 0:2], prob[:, :, 0:P], AX.X).then_inc(S["at_mx"], 1)
                dve.reduce_max(amx[:, 2:4], prob[:, :, P:3 * P], AX.X).then_inc(S["at_mx"], 1)
                dve.wait_ge(S["at_mx"], 2 * j + 2)
                dve.tensor_scalar(anb, amx, -0.125, None, ALU.mult).then_inc(S["at_nb"], 1)
                level(1)
                low(1)
                dve.wait_ge(S["at_p"], 4 * j + 4)
                dve.reciprocal(asum, asum).then_inc(S["at_rc"], 1)
                dve.wait_ge(S["at_rc"], 2 * j + 1)
                second = asum.rearrange("p (q c) -> p q c", c=2)[:, :, 1]
                dve.tensor_scalar(second, second, nlam, None, ALU.mult).then_inc(S["at_rc"], 1)
                dve.wait_ge(S["at_rc"], 2 * j + 2)
                for q, cols in ((0, slice(0, P)), (1, slice(P, 3 * P))):
                    dve.tensor_scalar(wq[:, cols], prob[:, 1, cols], asum[:, 2 * q + 1:2 * q + 2], None, ALU.mult).then_inc(S["at_w0"], 1)
                dve.wait_ge(S["at_w0"], 2 * j + 2)
                for q, cols in ((0, slice(0, P)), (1, slice(P, 3 * P))):
                    dve.scalar_tensor_tensor(wq[:, cols], prob[:, 0, cols], asum[:, 2 * q:2 * q + 1], wq[:, cols], ALU.mult, ALU.add).then_inc(S["at_w"], 1)
                level(2)
                low(2)
                level(3)
                dve.wait_ge(S["at_rs"], j + 1)
                dve.tensor_tensor(on, bank(3)[:, 0:256].rearrange("p (a b) -> p a b", a=2),
                                  ars.unsqueeze(2).broadcast_to([P, 2, P]), ALU.mult).then_inc(S["at_on"], 1)
                low(3)
                level(4)
                dve.wait_ge(S["at_oT"], j + 1)
                dve.tensor_scalar(atmp, bank(4)[:, 0:256], gn[:, G_SUB:G_SUB + 1], None, ALU.mult).then_inc(S["at_out"], 1)
                dve.wait_ge(S["at_out"], j + 1)
                dve.tensor_scalar(mh[:, j], atmp, 1.0, None, ALU.mult).then_inc(S["at_hi"], 1)
                dve.wait_ge(S["at_hi"], j + 1)
                dve.tensor_tensor(ml[:, j], atmp, mh[:, j].bitcast(F32), ALU.subtract).then_inc(S["at_end"], 1)
                low(4)
                level(5)
                level(6)
                low(5)
                waits(dve, j + 1, "rw_S", "rw_scl")
                dve.scalar_tensor_tensor(S0, bank(1)[:, P:2 * P], scl, head_ones, ALU.mult, ALU.mult).then_inc(S["rw_S0"], 1)
                dve.wait_ge(S["rw_y"], j + 1)
                y4 = bank(2)[:, 256:512].rearrange("p (a b) -> p a b", a=4)
                dve.reduce_sum(ymean, y4, AX.X).then_inc(S["rw_ymean"], 1)
                dve.wait_ge(S["rw_ymean"], 2 * j + 1)
                dve.tensor_scalar(ymean, ymean, 1.0 / 64, None, ALU.mult).then_inc(S["rw_ymean"], 1)
                dve.wait_ge(S["rw_ymean"], 2 * j + 2)
                dve.tensor_tensor(yc, y4, ymean.unsqueeze(2).broadcast_to([P, 4, 64]), ALU.subtract).then_inc(S["rw_yc"], 1)
                dve.wait_ge(S["rw_bonus"], j + 1)
                dve.tensor_tensor(rkb, bank(0)[:, 0:T], xm[:, 2], ALU.mult).then_inc(S["rw_bv"], 1)
                dve.wait_ge(S["rw_ysq"], j + 1)
                dve.reduce_sum(yvar, ysq, AX.X).then_inc(S["rw_yvar"], 1)
                waits(dve, j + 1, "rw_yrs", "rw_yc")
                dve.tensor_tensor(yc, yc, yrs.unsqueeze(2).broadcast_to([P, 4, 64]), ALU.mult).then_inc(S["rw_yn"], 1)
                waits(dve, j + 1, "rw_yTs", "rw_bv")
                dve.tensor_tensor(yT, yT, rkb, ALU.add).then_inc(S["rw_sum"], 1)
                waits(dve, j + 1, "rw_sum", "rw_g")
                dve.tensor_tensor(otmp, yT, bank(5)[:, 0:T], ALU.mult).then_inc(S["rw_out"], 1)
                dve.wait_ge(S["rw_out"], j + 1)
                dve.tensor_scalar(mh[:, NRW + j], otmp, 1.0, None, ALU.mult).then_inc(S["rw_hi"], 1)
                dve.wait_ge(S["rw_hi"], j + 1)
                dve.tensor_tensor(ml[:, NRW + j], otmp, mh[:, NRW + j].bitcast(F32), ALU.subtract).then_inc(S["rw_end"], 1)

            for u in range(6):
                for half in range(2):
                    Block(EVEN + u + 2).low(dve, half)
            even_step(0, [Block(EVEN + 6 + u) for u in range(8)])
            with dve.Fori(0, 3) as i:
                for e in range(2):
                    even_step(1 + 2 * i + e, [Block(EVEN + 12 + 6 * e + u, i, 12) for u in range(8)])
            even_step(7, None)

            def square(base, kt=KT, norm=None):
                def one(k, u, this, ahead):
                    if ahead is not None:
                        ahead.low(dve, 0)
                    product = this.result(dve)
                    dve.tensor_tensor(x[:, k], x[:, k], product, ALU.add).then_inc(evac_done, 1)
                    if ahead is not None:
                        ahead.low(dve, 1)
                    if norm is not None:
                        this.wait_evacuated(dve)
                        dve.tensor_tensor(nsq[:, u], x[:, k], x[:, k], ALU.mult).then_inc(S["sq"], 1)
                        add_square(norm, k, u)

                if norm is not None:
                    dve.memset(nss, 0.0).then_inc(S["sq_sum"], 1)
                at_end = base + KT == TOTAL
                with dve.Fori(0, KT // 4 - at_end) as i:
                    for u in range(4):
                        one(4 * i + u, u, Block(base + u, i, 4, kt=kt), Block(base + 2 + u, i, 4))
                for n in range(TOTAL - 4, TOTAL if at_end else 0):
                    one(n - base, n % 4, Block(n, kt=kt), Block(n + 2) if n + 2 < TOTAL else None)

            def ffn(layer, gain):
                norm(1 + 2 * layer, gain)
                first = FB * layer
                for m, (gate_up, down) in zip(PASSES, FFN[layer]):
                    with dve.Fori(0, m // 2) as i:
                        for b in range(2):
                            n = first + 2 * i + b
                            up = Block(gate_up + 2 * b + 1, i, 4)
                            for half in range(2):
                                Block(gate_up + 2 * b + 2, i, 4).low(dve, half)
                            Block(gate_up + 2 * b + 3, i, 4).low(dve, 0)
                            product = up.result(dve)
                            dve.wait_ge(evac_done, up.n + 2)
                            dve.tensor_tensor(hid32[:, b], sil[:, b], product, ALU.mult).then_inc(evac_done, 1)
                            up.wait_evacuated(dve)
                            dve.tensor_scalar(mh[:, 2 * i + b], hid32[:, b], 1.0, None, ALU.mult).then_inc(S["hid_high"], 1)
                            dve.wait_ge(S["hid_high"], n + 1)
                            dve.tensor_tensor(ml[:, 2 * i + b], hid32[:, b], mh[:, 2 * i + b].bitcast(F32), ALU.subtract).then_inc(S["hid_done"], 1)
                            Block(gate_up + 2 * b + 3, i, 4).low(dve, 1)
                    first += m
                    square(down, kt=m, norm=2 + 2 * layer if first == FB * layer + FB else None)

            dve.wait_ge(S["x_back"], 16)
            square(EVEN_OUT, norm=1)
            ffn(0, G_FFN0)
            norm(2, G_ATT1)

            base_mask = level_mask(1)
            dve.tensor_tensor(base_mask, base_mask, level_mask(0), ALU.add).then_inc(S["base_mask"], 1)
            dve.wait_ge(S["base_mask"], 1)
            dve.tensor_tensor(base_mask, base_mask, ident, ALU.add).then_inc(S["base_mask"], 1)
            dve.wait_ge(S["base_mask"], 2)

            def odd_step(h, last=False):
                def low(half):
                    if half < 4 or not last:
                        Block(ODD + 4 + half // 2, h, 4).low(dve, half % 2)

                def decays(l):
                    b = 2 << l
                    hv, dv = (t.rearrange("p (n s b) -> p n s b", s=2, b=b) for t in (hb, DD[:, l]))
                    ref = hv[:, :, 0, b - 1:b].broadcast_to([P, T // (2 * b), b])
                    dve.tensor_tensor(dv[:, :, 0], ref, hv[:, :, 0], ALU.subtract).then_inc(S["hg_D"], 1)
                    if b < P:
                        dve.tensor_tensor(dv[:, :, 1], hv[:, :, 1], ref, ALU.subtract).then_inc(S["hg_D"], 1)
                    else:
                        dve.tensor_scalar(dv[:, :, 1], hv[:, :, 1], 1.0, None, ALU.mult).then_inc(S["hg_D"], 1)

                def decayed(l):
                    b = 2 << l
                    for s, src in ((0, hk), (1, hq)):
                        part = [t.rearrange("p (n s b) -> p n s b", s=2, b=b)[:, :, s] for t in (XX[:, l], DD[:, l], src)]
                        dve.tensor_tensor(*part, ALU.mult).then_inc(S["hg_X"], 1)

                dve.wait_ge(S["hg_end"], h + 1)
                dve.wait_ge(S["hg_sig"], 2 * h + 2)
                dve.tensor_tensor(gs, gsig, hg, ALU.mult).then_inc(S["hg_silu"], 1)
                dve.wait_ge(S["hg_lf"], h + 1)
                for c in range(2):
                    dve.tensor_tensor_scan(hb[:, c * P:(c + 1) * P], ones, lf[:, c * P:(c + 1) * P], 0.0, ALU.mult, ALU.add).then_inc(S["hg_b"], 1)
                dve.scalar_tensor_tensor(hk, fs, hpar[:, 1:2], hpar[:, 1:2].broadcast_to([P, T]), ALU.mult, ALU.subtract,
                                         reverse1=True).then_inc(S["hg_k"], 1)
                low(2)
                dve.wait_ge(S["hg_b"], 2 * h + 2)
                hv, dv = (t.rearrange("p (n b) -> p n b", b=4) for t in (hb, DD[:, 0]))
                dve.tensor_tensor(dv, hv, hv[:, :, 1:2].broadcast_to([P, T // 4, 4]), ALU.subtract).then_inc(S["hg_D"], 1)
                for l in range(1, 7):
                    decays(l)
                waits(dve, h + 1, "hg_k")
                if not last:
                    lower_bound(h + 1)
                low(3)
                dve.wait_ge(S["hg_E"], 3 * h + 2)
                evacuated(dve, ODD + 4 * h + 3)
                dve.tensor_tensor(XX[:, 0], DD[:, 0], hq, ALU.mult).then_inc(S["hg_X"], 1)
                dve.tensor_tensor(XX[:, 7], DD[:, 7], hk, ALU.mult).then_inc(S["hg_X"], 1)
                for l in range(1, 4):
                    decayed(l)
                low(4)
                dve.wait_ge(S["hg_E"], 3 * h + 3)
                for l in range(4, 7):
                    decayed(l)
                low(5)
                low(6)
                dve.wait_ge(S["hg_mm"], h + 1)
                masks = cst[:, C_LVL + P:C_LVL + 7 * P].rearrange("p (l t) -> p l t", t=P)
                p4 = pm[:, 0:6 * T].rearrange("p (l c t) -> p l c t", l=6, c=2)
                a4 = AM.rearrange("p l (c t) -> p l c t", c=2)
                for c in range(2):
                    dve.tensor_tensor(a4[:, :, c], p4[:, :, c], masks, ALU.mult).then_inc(S["hg_AM"], 1)
                dve.tensor_copy(A01, bank(4)[:, 0:P]).then_inc(S["hg_A01"], 1)
                dve.wait_ge(S["hg_AM"], 2 * h + 2)
                for n, (to, at, w) in enumerate(((0, 3, 3), (0, 1, 1), (0, 2, 1))):
                    dve.tensor_tensor(AM[:, to:to + w], AM[:, to:to + w], AM[:, at:at + w], ALU.add).then_inc(S["hg_AT"], 1)
                    dve.wait_ge(S["hg_AT"], 3 * h + n + 1)
                low(7)
                low(8)
                dve.wait_ge(S["hg_rs"], h + 1)
                dve.tensor_tensor(hon, bank(5)[:, 256:512].rearrange("p (a b) -> p a b", a=2),
                                  ars.unsqueeze(2).broadcast_to([P, 2, P]), ALU.mult).then_inc(S["hg_on"], 1)
                low(9)
                dve.wait_ge(S["hg_oT"], h + 1)
                dve.scalar_tensor_tensor(htmp, bank(4)[:, 256:512], gn[:, G_HGN:G_HGN + 1], gs, ALU.mult, ALU.mult).then_inc(S["hg_out"], 1)
                dve.wait_ge(S["hg_out"], h + 1)
                dve.tensor_scalar(mh[:, h], htmp, 1.0, None, ALU.mult).then_inc(S["hg_hi"], 1)
                dve.wait_ge(S["hg_hi"], h + 1)
                dve.tensor_tensor(ml[:, h], htmp, mh[:, h].bitcast(F32), ALU.subtract).then_inc(S["hg_end"], 1)

            def lower_bound(h):
                dve.tensor_scalar(hpar[:, 0:1], hlb[:, h:h + 1] if isinstance(h, int) else hlb[:, bass.ds(h, 1)], 1.0, None, ALU.mult).then_inc(S["hg_par"], 1)
                dve.tensor_scalar(hpar[:, 1:2], homl[:, h:h + 1] if isinstance(h, int) else homl[:, bass.ds(h, 1)], 1.0, None, ALU.mult).then_inc(S["hg_par"], 1)

            for u in range(3):
                for half in range(2):
                    Block(ODD + u + 2).low(dve, half)
            lower_bound(0)
            dve.wait_ge(S["hg_par"], 2)
            with dve.Fori(0, NHG - 1) as h:
                odd_step(h)
            odd_step(NHG - 1, last=True)
            square(ODD_OUT, norm=3)
            ffn(1, G_FFN1)
            norm(4, G_FIN)

        @block.tensor
        def _(pe):
            def norm(m):
                pe.wait_ge(S["sq_sum"], (m + 1) * (KT + 1))
                pe.matmul(bank(0)[:, 0:T], ones, nss, start=True, stop=True).then_inc(S["sq_total"], 1)
                if m < 4:
                    first = (LOWRANK, FFN[0][0][0], ODD, FFN[1][0][0])[m]
                    for k in range(KT):
                        pe.wait_ge(S["h_low"], m * KT + k + 1)
                        Block(first).tile(pe, k, hh, hl, (1, 2))
                        Block(first + 1).tile(pe, k, hh, hl, (0, 1))

            def transposed(out, src):
                return pe.transpose(out, src, ident)

            pe.sem_inc(half_done, 2 * RES)
            pe.sem_inc(evac_done, 2)
            pe.wait_ge(S["consts_in"], 32)
            norm(0)
            for n in range(LOWRANK + 2, EVEN + 6):
                for half in range(2):
                    Block(n).products(pe, half, hh, hl)

            def even_step(j, blocks):
                def dense(h):
                    if blocks is not None:
                        blocks[h // 2].products(pe, h % 2, hh, hl)

                waits(pe, j + 1, "rw_end", "at_end")
                pe.wait_ge(S["low_acts"], 3)
                pe.wait_ge(S["rw_par"], 32 * j + 32)
                pe.matmul(bank(5)[:, 0:T], wa[0:64], thw[0:64], start=True, stop=True)
                pe.matmul(bank(0)[:, 0:T], wa[64:128], thw[64:128], start=True, stop=True).then_inc(S["rw_za"], 1)
                evacuated(pe, EVEN + 6 * j + 5)
                pe.matmul(bank(3), rot, flat(aqk), start=True, stop=True).then_inc(S["at_rot"], 1)
                dense(0)
                pe.wait_ge(S["rw_sq"], j + 1)
                pe.matmul(bank(2)[:, 0:T], head_ones, d3[:, 2], start=True, stop=True).then_inc(S["rw_ss"], 1)
                pe.wait_ge(S["rw_xv"], j + 1)
                for c in range(2):
                    last = transposed(bank(4)[:, 256 + c * P:256 + (c + 1) * P], xm[:, 2, c * P:(c + 1) * P])
                last.then_inc(S["rw_vt"], 1)
                dense(1)
                waits(pe, j + 1, "rw_at", "rw_bt", "rw_rt", "rw_kt", "rw_sig", "rw_a")
                hc = [(h, c) for h in range(2) for c in range(2)]
                for n, (h, c) in enumerate(hc):
                    rows, cols = slice(64 * h, 64 * h + 64), slice(c * P, (c + 1) * P)
                    last = pe.matmul(bank(n // 2)[:, (n % 2) * 256:(n % 2) * 256 + 256], bk[rows, 0, cols],
                                     AR[rows, c].rearrange("p a b -> p (a b)"), start=True, stop=True)
                last.then_inc(S["rw_m1"], 1)
                pe.wait_ge(S["rw_vn"], j + 1)
                for n, (h, c) in enumerate(hc):
                    rows, cols = slice(64 * h, 64 * h + 64), slice(c * P, (c + 1) * P)
                    last = pe.matmul(bank(5 - h)[:, c * P:(c + 1) * P], AR[rows, c, 0], bk[rows, 0, cols], start=True, stop=True)
                last.then_inc(S["rw_m3"], 1)
                waits(pe, j + 1, "at_sin", "rw_ssmax")
                for n, (h, c) in enumerate(hc):
                    rows, cols = slice(64 * h, 64 * h + 64), slice(c * P, (c + 1) * P)
                    last = pe.matmul(bank(2 + n // 2)[:, (n % 2) * 256:(n % 2) * 256 + 256], bk[rows, 1, cols],
                                     AR[rows, c].rearrange("p a b -> p (a b)"), start=True, stop=True)
                last.then_inc(S["rw_m2"], 1)
                dense(2)
                pe.wait_ge(S["rw_T0"], 3 * j + 2)
                waits(pe, j + 1, "at_qk")
                for c in range(2):
                    rows = slice(64 * c, 64 * c + 64)
                    pe.matmul(bank(4 + c)[:, 0:P], qk[rows, 0, 0:P], qk[rows, 1, 0:P], start=True, stop=True)
                    last = pe.matmul(bank(4 + c)[:, P:3 * P], qk[rows, 0, P:T], qk[rows, 1], start=True, stop=True)
                last.then_inc(S["at_s"], 1)

                def z(l):
                    pe.wait_ge(S["rw_X"], 6 * j + l)
                    pe.wait_ge(S["rw_TT"], 7 * j + l)
                    if l == 1:
                        pe.wait_ge(S["rw_KTR"], 2 * j + 2)
                    for n in range(4):
                        last = pe.matmul(bank(2)[:, n * P:(n + 1) * P], Xb[:, l % 2, n], TT[:, n, 0], start=True, stop=True)
                    last.then_inc(S["rw_Z"], 1)

                def txt(l):
                    pe.wait_ge(S["rw_Zs"], 6 * j + l)
                    for n in range(4):
                        o = bank(0, 2)[:, n * 256:(n + 1) * 256]
                        if l < LEVELS - 1:
                            pe.matmul(o[:, 0:P], TT[:, n, 1], Zs[:, n], start=True, stop=True)
                        last = pe.matmul(o[:, P:2 * P], Zs[:, n], TT[:, n, 1], start=True, stop=True)
                    last.then_inc(S["rw_TXT"], 1)

                z(1)
                dense(3)
                txt(1)
                dense(4)
                z(2)
                pe.wait_ge(S["at_sm"], 2 * j + 2)
                for c in range(2):
                    last = transposed(bank(4)[:, c * P:(c + 1) * P], av[:, c * P:(c + 1) * P])
                last.then_inc(S["at_vT"], 1)
                pe.wait_ge(S["at_w"], 2 * j + 2)
                for n in range(3):
                    last = transposed(bank(3)[:, n * P:(n + 1) * P], wq[:, n * P:(n + 1) * P])
                last.then_inc(S["at_wT"], 1)
                txt(2)
                dense(5)
                z(3)
                waits(pe, j + 1, "at_wt", "at_vn")
                pe.matmul(bank(3)[:, 0:P], wt[:, 0:P], avn[:, 0], start=True, stop=True)
                pe.matmul(bank(3)[:, P:2 * P], wt[:, P:2 * P], avn[:, 0], start=True, stop=False)
                pe.matmul(bank(3)[:, P:2 * P], wt[:, 2 * P:3 * P], avn[:, 1], start=False, stop=True).then_inc(S["at_o"], 1)
                dense(6)
                txt(3)
                dense(7)
                z(4)
                pe.wait_ge(S["at_on"], j + 1)
                for q in range(2):
                    last = transposed(bank(4)[:, q * P:(q + 1) * P], on[:, q])
                last.then_inc(S["at_oT"], 1)
                dense(8)
                txt(4)
                z(5)
                dense(9)
                txt(5)
                transposed(bank(5)[:, 0:P], bk[:, 1, 0:P])
                transposed(bank(5)[:, P:2 * P], bk[:, 0, 0:P]).then_inc(S["rw_kbT"], 1)
                dense(10)
                z(6)
                pe.wait_ge(S["rw_kbn"], j + 1)
                for h in range(2):
                    last = pe.matmul(bank(5)[:, 256 + 64 * h:320 + 64 * h], KTR[:, 2 * h, 0:P], Vn[:, 0, 64 * h:64 * h + 64], start=True, stop=True)
                last.then_inc(S["rw_R0"], 1)
                txt(6)
                dense(11)
                pe.wait_ge(S["rw_TT"], 7 * j + 7)
                pe.wait_ge(S["rw_nR0"], j + 1)
                for h in range(2):
                    last = pe.matmul(bank(5)[:, 384 + 64 * h:448 + 64 * h], TT[:, 2 * h, 1], nR[:, 0, 64 * h:64 * h + 64], start=True, stop=True)
                last.then_inc(S["rw_U0"], 1)
                pe.wait_ge(S["rw_Us0"], j + 1)
                pe.matmul(bank(1)[:, P:2 * P], kbn[:, 0], Vn[:, 0], start=True, stop=False)
                pe.matmul(bank(1)[:, P:2 * P], kbn[:, 1], Us[:, 0], start=False, stop=True).then_inc(S["rw_S"], 1)
                for h in range(2):
                    o, v = bank(2)[:, 256 + 64 * h:320 + 64 * h], slice(64 * h, 64 * h + 64)
                    pe.matmul(o, KTR[:, 2 * h, P:2 * P], Vn[:, 0, v], start=True, stop=False)
                    pe.matmul(o, LTR[:, 2 * h, P:2 * P], Us[:, 0, v], start=False, stop=True)
                pe.wait_ge(S["rw_S0"], j + 1)
                pe.matmul(bank(1)[:, 0:P], AR[:, 1, 0], S0, start=True, stop=False, skip_group_check=True)
                for h in range(2):
                    last = pe.matmul(bank(1)[:, 64 * h:64 * h + 64], KTR[:, 2 * h + 1, 0:P], Vn[:, 1, 64 * h:64 * h + 64],
                                     start=False, stop=True, skip_group_check=True)
                last.then_inc(S["rw_R1"], 1)
                pe.wait_ge(S["rw_nR1"], j + 1)
                for h in range(2):
                    last = pe.matmul(bank(2)[:, 64 * h:64 * h + 64], TT[:, 2 * h + 1, 1], nR[:, 1, 64 * h:64 * h + 64], start=True, stop=True)
                last.then_inc(S["rw_U1"], 1)
                pe.wait_ge(S["rw_Us1"], j + 1)
                pe.matmul(bank(2)[:, 384:512], AR[:, 1, 1], S0, start=True, stop=False, skip_group_check=True)
                for h in range(2):
                    o, v = bank(2)[:, 384 + 64 * h:448 + 64 * h], slice(64 * h, 64 * h + 64)
                    pe.matmul(o, KTR[:, 2 * h + 1, P:2 * P], Vn[:, 1, v], start=False, stop=False, skip_group_check=True)
                    last = pe.matmul(o, LTR[:, 2 * h + 1, P:2 * P], Us[:, 1, v], start=False, stop=True, skip_group_check=True)
                last.then_inc(S["rw_y"], 1)
                pe.matmul(bank(0)[:, 0:T], head_ones, rkb, start=True, stop=True).then_inc(S["rw_bonus"], 1)
                pe.wait_ge(S["rw_late"], 32 * j + 32)
                pe.matmul(bank(5)[:, 0:T], gu[0:32], sgl[0:32], start=True, stop=True).then_inc(S["rw_g"], 1)
                pe.wait_ge(S["rw_yn"], j + 1)
                for c in range(2):
                    last = transposed(bank(1)[:, 256 + c * P:256 + (c + 1) * P], flat(yc)[:, c * P:(c + 1) * P])
                last.then_inc(S["rw_yT"], 1)

            even_step(0, [Block(EVEN + 6 + u) for u in range(6)])
            with pe.Fori(0, 3) as i:
                for e in range(2):
                    even_step(1 + 2 * i + e, [Block(EVEN + 12 + 6 * e + u, i, 12) for u in range(6)])
            even_step(7, None)

            def run(base, rounds, high, low, kt=KT, skip=0):
                if rounds == 1:
                    for n in range(base + skip, base + 4):
                        for half in range(2):
                            Block(n, kt=kt).products(pe, half, high, low)
                    return
                with pe.Fori(0, rounds) as i:
                    for u in range(4):
                        for half in range(2):
                            Block(base + u, i, 4, kt=kt).products(pe, half, high, low)

            def ffn(layer):
                norm(1 + 2 * layer)
                first = FB * layer
                for m, (gate_up, down) in zip(PASSES, FFN[layer]):
                    if gate_up == FFN[layer][0][0]:
                        run(gate_up, 1, hh, hl, skip=2)
                        run(gate_up + 4, m // 2 - 1, hh, hl)
                    else:
                        run(gate_up, m // 2, hh, hl)
                    first += m
                    pe.wait_ge(S["hid_done"], first)
                    run(down, KT // 4, mh, ml, kt=m)

            waits(pe, NRW + 1, "rw_end", "at_end")
            run(EVEN_OUT, KT // 4, mh, ml)
            ffn(0)
            norm(2)

            def odd_step(h, last=False):
                def dense(first, end):
                    for k in range(first, 0 if last else end):
                        Block(ODD + 4 + k // KT, h, 4).tile(pe, k % KT, hh, hl)

                pe.wait_ge(S["hg_end"], h + 1)
                evacuated(pe, ODD + 4 * h + 1)
                for c in range(2):
                    prod = transposed(bank(5)[:, c * P:(c + 1) * P], hi[:, c * P:(c + 1) * P])
                prod.then_inc(S["hg_iT"], 1)
                dense(0, 32)
                pe.wait_ge(S["hg_X"], 14 * h + 14)
                pe.matmul(bank(4)[:, 0:P], XX[:, 6, 0:P], XX[:, 6, P:T], start=True, stop=True)
                for l in range(6):
                    for c in range(2):
                        cols = slice(c * P, (c + 1) * P)
                        prod = pe.matmul(pm[:, l * T + c * P:l * T + (c + 1) * P], XX[:, l or 7, cols], XX[:, l, cols], start=True, stop=True)
                prod.then_inc(S["hg_mm"], 1)
                dense(32, 46)
                pe.wait_ge(S["hg_AT"], 3 * h + 3)
                waits(pe, h + 1, "hg_A01", "hg_In")
                pe.matmul(bank(5)[:, 256:384], AM[:, 0, 0:P], In[:, 0], start=True, stop=True)
                pe.matmul(bank(5)[:, 384:512], A01, In[:, 0], start=True, stop=False)
                pe.matmul(bank(5)[:, 384:512], AM[:, 0, P:T], In[:, 1], start=False, stop=True).then_inc(S["hg_o"], 1)
                dense(46, 54)
                pe.wait_ge(S["hg_on"], h + 1)
                for q in range(2):
                    prod = transposed(bank(4)[:, 256 + q * P:256 + (q + 1) * P], hon[:, q])
                prod.then_inc(S["hg_oT"], 1)
                dense(54, 64)

            for n in range(2, 4):
                for half in range(2):
                    Block(ODD + n).products(pe, half, hh, hl)
            with pe.Fori(0, NHG - 1) as h:
                odd_step(h)
            odd_step(NHG - 1, last=True)
            pe.wait_ge(S["hg_end"], NHG + 1)
            run(ODD_OUT, KT // 4, mh, ml)
            ffn(1)
            norm(4)


def kernel(x, attn_norm_g, ffn_norm_g, final_norm_g, even_w_in, even_w_out, da_lambda, da_subln_g, rw_mu, rw_w0,
           rw_w_up, rw_a0, rw_a_up, rw_g_up, rw_k_k, rw_k_a, rw_r_k, rw_ln_w, rw_ln_b, odd_w_in, odd_w_out,
           hg_lower_bound, hg_norm_g, ffn_w_gate, ffn_w_up, ffn_w_down):
    import concourse.bacc as bacc
    from concourse.bass_utils import run_bass_kernel_spmd as run

    a = np.asarray

    def blocks(w):
        w = a(w)
        return w.reshape(w.shape[0] // P, P, w.shape[1] // P, P).transpose(2, 1, 0, 3)

    def columns(v):
        return a(v).reshape(-1, P).T

    we = a(even_w_in[0])
    lowrank = blocks(np.concatenate([we[:, 6144:6304], np.zeros((D, 96), np.float32)], 1))
    cols = [blocks(we[:, n * 1024:(n + 1) * 1024]) for n in range(6)]
    order = [cols[g][j] for j in range(NRW) for g in (3, 4, 5, 0, 1, 2)]
    w_even = np.concatenate([lowrank, np.stack(order)])
    wo = blocks(odd_w_in[0]).reshape(4, NHG, P, KT, P)
    w_odd = wo[[1, 2, 3, 0]].transpose(1, 0, 2, 3, 4).reshape(4 * NHG, P, KT, P)
    w_gu = np.stack([np.stack([blocks(ffn_w_gate[i]), blocks(ffn_w_up[i])], 1).reshape(2 * FB, P, KT, P) for i in range(2)])
    w_down = np.stack([blocks(ffn_w_down[i]) for i in range(2)])
    mu = a(rw_mu[0])
    gains = np.zeros((P, NG), np.float32)
    for at, v in ((G_ATT0, attn_norm_g[0]), (G_FFN0, ffn_norm_g[0]), (G_ATT1, attn_norm_g[1]), (G_FFN1, ffn_norm_g[1]),
                  (G_FIN, final_norm_g), (G_LB0, hg_lower_bound[0]), (G_LB1, hg_lower_bound[1]), (G_SUB, da_subln_g[0]),
                  (G_HGN, hg_norm_g[0]), (G_MUW, mu[3072:3200])):
        c = columns(v)
        gains[:, at:at + c.shape[1]] = c
    gains[0:32, G_MUG] = mu[3200:3232]
    gains[:, G_LAM:G_LAM + 256] = a(da_lambda[0]).reshape(1, 256)
    par = np.stack([columns(v) for v in (mu[0:1024], mu[1024:2048], mu[2048:3072], rw_w0[0], rw_a0[0], rw_k_k[0], rw_k_a[0],
                                         a(rw_r_k[0]).reshape(-1))], 2).transpose(1, 0, 2)
    par_ln = np.stack([columns(rw_ln_w[0]), columns(rw_ln_b[0])], 2).transpose(1, 0, 2)
    wa_up = np.concatenate([a(rw_w_up[0]), a(rw_a_up[0])], 0).reshape(P, NRW, P).transpose(1, 0, 2)
    g_up = a(rw_g_up[0]).reshape(32, NRW, P).transpose(1, 0, 2)
    arrays = {
        "xT": a(x)[0].T.reshape(KT, P, T).transpose(1, 0, 2), "w_even": w_even, "w_even_out": blocks(even_w_out[0]),
        "w_odd": w_odd, "w_odd_out": blocks(odd_w_out[0]), "w_gu": w_gu, "w_down": w_down,
        "consts": shape_constants(), "gains": gains, "par": par, "par_ln": par_ln, "wa_up": wa_up, "g_up": g_up,
    }
    arrays = {k: np.ascontiguousarray(v) for k, v in arrays.items()}
    nc = bacc.Bacc("TRN2", target_bir_lowering=False, num_devices=1)
    aps = {k: nc.dram_tensor(k, v.shape, F32, kind="ExternalInput").ap() for k, v in arrays.items()}
    out = nc.dram_tensor("out", (P, KT, T), F32, kind="ExternalOutput").ap()
    build(nc, *(aps[k] for k in arrays), out)
    r = run(nc, [arrays], core_ids=[0])
    return np.ascontiguousarray(a(r.results[0]["out"]).transpose(1, 0, 2).reshape(D, T).T.reshape(1, T, D))
```
